# Optimizing a Trainium2 kernel written in Bass

```python
import jax
import jax.numpy as jnp
from jax import lax
import numpy as np

D_MODEL = 1024
BATCH = 1
SEQ = 256
DEPTH = 2

D_FF = 2816
A_HEADS = 8
A_KV_HEADS = 2
A_HEAD_DIM = 64
WINDOW = 128
A_BLOCK = 128
B_HEADS = 4
B_KEY_DIM = 128
B_VAL_DIM = 128
B_CHUNK = 64
C_HEADS = 16
C_Q_RANK = 256
C_KV_RANK = 256
C_NOPE = 64
C_ROPE = 32
C_V = 64
C_QBLOCK = 128
ROPE_THETA = 10000.0
LN_EPS = 1e-5
RMS_EPS = 1e-6
DEEPNORM_ALPHA = (2 * DEPTH) ** 0.25
DEEPNORM_BETA = (8 * DEPTH) ** -0.25
N_EVEN = (DEPTH + 1) // 2
N_ODD = DEPTH // 2
N_SUB = 3
A_Q_W = A_HEADS * A_HEAD_DIM
A_KV_W = A_KV_HEADS * A_HEAD_DIM
B_K_W = B_HEADS * B_KEY_DIM
B_V_W = B_HEADS * B_VAL_DIM
HYB_SPLITS = (A_Q_W, A_KV_W, A_KV_W, B_K_W, B_K_W, B_K_W, B_V_W, B_V_W)
HYB_IN = sum(HYB_SPLITS)
HYB_OUT = A_Q_W + B_V_W
MLA_DOWN = C_Q_RANK + C_KV_RANK + C_ROPE
F32 = jnp.float32

kernel_name = 'hybrid_swa_hgrn2_mla_macaron_deepnorm_adaln'

def layer_norm(x, g, b):
    xf = x.astype(F32)
    mu = jnp.mean(xf, -1, keepdims=True)
    var = jnp.mean(jnp.square(xf - mu), -1, keepdims=True)
    return ((xf - mu) * lax.rsqrt(var + LN_EPS) * g + b).astype(x.dtype)

def rms_norm(x, w):
    xf = x.astype(F32)
    return (xf * lax.rsqrt(jnp.mean(xf * xf, -1, keepdims=True) + RMS_EPS) * w).astype(x.dtype)

def swiglu(h, w_gate, w_up, w_down):
    return (jax.nn.silu(h @ w_gate) * (h @ w_up)) @ w_down

def rope(x, pos):
    half = x.shape[-1] // 2
    freqs = ROPE_THETA ** (-jnp.arange(half, dtype=F32) / half)
    ang = pos.astype(F32)[..., None] * freqs
    ang = ang.reshape(ang.shape[:2] + (1,) * (x.ndim - 3) + (half,))
    cos, sin = jnp.cos(ang), jnp.sin(ang)
    x1, x2 = x[..., :half].astype(F32), x[..., half:].astype(F32)
    return jnp.concatenate([x1 * cos - x2 * sin, x1 * sin + x2 * cos], -1).astype(x.dtype)

def alibi_slopes(n):
    return 2.0 ** (-8.0 * jnp.arange(1, n + 1, dtype=F32) / n)

def window_attention(q, k, v, pos, sink):
    bsz, seq = q.shape[:2]
    nb = seq // A_BLOCK
    grp = A_HEADS // A_KV_HEADS

    def band(t):
        tp = jnp.pad(t, [(0, 0), (A_BLOCK, A_BLOCK)] + [(0, 0)] * (t.ndim - 2))
        tb = tp.reshape((bsz, nb + 2, A_BLOCK) + t.shape[2:])
        return jnp.concatenate([tb[:, :-2], tb[:, 1:-1], tb[:, 2:]], axis=2)

    kb, vb, pk = band(k), band(v), band(pos)
    qb = q.reshape(bsz, nb, A_BLOCK, A_KV_HEADS, grp, A_HEAD_DIM)
    pq = pos.reshape(bsz, nb, A_BLOCK)
    s = jnp.einsum('bnqhgd,bnkhd->bnhgqk', qb, kb).astype(F32) * (A_HEAD_DIM ** -0.5)
    qi = jnp.arange(A_BLOCK)[:, None] + A_BLOCK
    ki = jnp.arange(3 * A_BLOCK)[None, :]
    abs_k = jnp.arange(nb)[:, None, None] * A_BLOCK + ki[None] - A_BLOCK
    valid = (jnp.abs(qi - ki) <= WINDOW)[None] & (abs_k >= 0) & (abs_k < seq)
    dist = jnp.abs(pq[..., :, None] - pk[..., None, :]).astype(F32)
    slopes = alibi_slopes(A_HEADS).reshape(A_KV_HEADS, grp)[None, None, :, :, None, None]
    s = s - slopes * dist[:, :, None, None]
    s = jnp.where(valid[None, :, None, None], s, -jnp.inf)
    sink_l = sink.astype(F32).reshape(A_KV_HEADS, grp)[None, None, :, :, None, None]
    m = jnp.maximum(jnp.max(s, -1, keepdims=True), sink_l)
    p = jnp.exp(s - m)
    p = p / (jnp.sum(p, -1, keepdims=True) + jnp.exp(sink_l - m))
    o = jnp.einsum('bnhgqk,bnkhd->bnqhgd', p.astype(v.dtype), vb)
    return o.reshape(bsz, seq, A_Q_W)

def hgrn2_scan(q, k, v, logf):
    bsz, nh, seq, dk = q.shape
    dv = v.shape[-1]
    n = seq // B_CHUNK
    q, k, logf = [t.reshape(bsz, nh, n, B_CHUNK, dk) for t in (q, k, logf)]
    v = v.reshape(bsz, nh, n, B_CHUNK, dv)
    b = jnp.cumsum(logf, axis=3)
    b_mid = b[:, :, :, B_CHUNK // 2 - 1:B_CHUNK // 2]
    b_end = b[:, :, :, -1:]
    a = jnp.einsum('bhnck,bhnsk->bhncs', q * jnp.exp(b - b_mid), k * jnp.exp(b_mid - b))
    tri = jnp.tril(jnp.ones((B_CHUNK, B_CHUNK), bool))
    o_intra = jnp.einsum('bhncs,bhnsv->bhncv', jnp.where(tri, a, 0.0), v)
    d_state = jnp.einsum('bhnck,bhncv->bhnkv', k * jnp.exp(b_end - b), v)
    decay = jnp.exp(b_end[:, :, :, 0])

    def step(s_prev, inp):
        dec, ds = inp
        return dec[..., None] * s_prev + ds, s_prev

    _, s0 = lax.scan(step, jnp.zeros((bsz, nh, dk, dv), q.dtype),
                     (jnp.moveaxis(decay, 2, 0), jnp.moveaxis(d_state, 2, 0)))
    s0 = jnp.moveaxis(s0, 0, 2)
    o_inter = jnp.einsum('bhnck,bhnkv->bhncv', q * jnp.exp(b), s0)
    return (o_intra + o_inter).reshape(bsz, nh, seq, dv)

def hgrn2_bidir(hq, hff, hfb, hi, hg, lb, norm_w):
    bsz, seq = hq.shape[:2]

    def heads(t, d):
        return t.reshape(bsz, seq, B_HEADS, d).transpose(0, 2, 1, 3).astype(F32)

    q = jax.nn.silu(heads(hq, B_KEY_DIM))
    v = heads(hi, B_VAL_DIM)
    lbh = lb.astype(F32).reshape(B_HEADS, 1, B_KEY_DIM)

    def gates(hf):
        f = lbh + (1.0 - lbh) * jax.nn.sigmoid(heads(hf, B_KEY_DIM))
        return 1.0 - f, jnp.log(f)

    k_f, g_f = gates(hff)
    k_b, g_b = gates(hfb)
    flip = lambda t: jnp.flip(t, axis=2)
    o = hgrn2_scan(q, k_f, v, g_f) + flip(hgrn2_scan(flip(q), flip(k_b), flip(v), flip(g_b)))
    o = rms_norm(o, norm_w[:, None, :])
    o = o.transpose(0, 2, 1, 3).reshape(bsz, seq, B_V_W).astype(hg.dtype)
    return o * jax.nn.silu(hg)

def hybrid_mixer(h, pos, w_in, w_out, sink, lb, norm_w):
    bsz, seq, _ = h.shape
    offs = [int(o) for o in np.cumsum(HYB_SPLITS)[:-1]]
    aq, ak, av, bq, bff, bfb, bi, bg = jnp.split(h @ w_in, offs, axis=-1)
    o_a = window_attention(aq.reshape(bsz, seq, A_HEADS, A_HEAD_DIM),
                           ak.reshape(bsz, seq, A_KV_HEADS, A_HEAD_DIM),
                           av.reshape(bsz, seq, A_KV_HEADS, A_HEAD_DIM), pos, sink)
    o_b = hgrn2_bidir(bq, bff, bfb, bi, bg, lb, norm_w)
    return jnp.concatenate([o_a, o_b], axis=-1) @ w_out

def mla(h, pos, w_down, q_norm, kv_norm, w_uq, w_ukv, w_out):
    bsz, seq, _ = h.shape
    cq, ckv, kr = jnp.split(h @ w_down, [C_Q_RANK, C_Q_RANK + C_KV_RANK], axis=-1)
    q = (rms_norm(cq, q_norm) @ w_uq).reshape(bsz, seq, C_HEADS, C_NOPE + C_ROPE)
    q_nope, q_rope = q[..., :C_NOPE], rope(q[..., C_NOPE:], pos)
    kv = (rms_norm(ckv, kv_norm) @ w_ukv).reshape(bsz, seq, C_HEADS, C_NOPE + C_V)
    k_nope, v = kv[..., :C_NOPE], kv[..., C_NOPE:]
    k_rope = rope(kr, pos)
    scale = (C_NOPE + C_ROPE) ** -0.5
    nq = seq // C_QBLOCK
    qn_b = q_nope.reshape(bsz, nq, C_QBLOCK, C_HEADS, C_NOPE).swapaxes(0, 1)
    qr_b = q_rope.reshape(bsz, nq, C_QBLOCK, C_HEADS, C_ROPE).swapaxes(0, 1)

    def block(args):
        qn_i, qr_i = args
        s = (jnp.einsum('bqhd,bkhd->bhqk', qn_i, k_nope)
             + jnp.einsum('bqhr,bkr->bhqk', qr_i, k_rope)).astype(F32) * scale
        p = jax.nn.softmax(s, axis=-1).astype(v.dtype)
        return jnp.einsum('bhqk,bkhd->bqhd', p, v)

    o = lax.map(block, (qn_b, qr_b))
    return o.swapaxes(0, 1).reshape(bsz, seq, C_HEADS * C_V) @ w_out

def modulated_sublayer(x, mod, g, b, fn, res_w):
    shift, scale, gate = mod[:, 0, None, :], mod[:, 1, None, :], mod[:, 2, None, :]
    y = fn(x * (1.0 + scale) + shift)
    return layer_norm(DEEPNORM_ALPHA * x + res_w * (1.0 + gate) * y, g, b)

def setup_inputs(seed: int = 0) -> dict:
    key = jax.random.key(seed)
    ks = jax.random.split(key, 24)
    nrm = lambda k, shape, s: jax.random.normal(k, shape, F32) * s
    d = D_MODEL
    return {
        'x': nrm(ks[0], (BATCH, SEQ, d), 1.0),
        'c': nrm(ks[1], (BATCH, d), 1.0),
        'positions': jnp.broadcast_to(jnp.arange(SEQ, dtype=jnp.int32), (BATCH, SEQ)),
        'ada_w': nrm(ks[2], (DEPTH, d, N_SUB * 3 * d), 0.1 * d ** -0.5),
        'ada_b': nrm(ks[3], (DEPTH, N_SUB * 3 * d), 0.01),
        'ln_g': 1.0 + nrm(ks[4], (DEPTH, N_SUB, d), 0.01),
        'ln_b': nrm(ks[5], (DEPTH, N_SUB, d), 0.01),
        'ffn_w_gate': nrm(ks[6], (DEPTH, 2, d, D_FF), d ** -0.5),
        'ffn_w_up': nrm(ks[7], (DEPTH, 2, d, D_FF), d ** -0.5),
        'ffn_w_down': nrm(ks[8], (DEPTH, 2, D_FF, d), DEEPNORM_BETA * D_FF ** -0.5),
        'hyb_w_in': nrm(ks[9], (N_EVEN, d, HYB_IN), d ** -0.5),
        'hyb_w_out': nrm(ks[10], (N_EVEN, HYB_OUT, d), DEEPNORM_BETA * HYB_OUT ** -0.5),
        'attn_sink': nrm(ks[11], (N_EVEN, A_HEADS), 0.5),
        'hgrn_lb_logits': nrm(ks[12], (DEPTH + 1, B_K_W), 0.1),
        'hgrn_norm_w': 1.0 + nrm(ks[13], (N_EVEN, B_HEADS, B_VAL_DIM), 0.01),
        'mla_w_down': nrm(ks[14], (N_ODD, d, MLA_DOWN), d ** -0.5),
        'mla_q_norm': 1.0 + nrm(ks[15], (N_ODD, C_Q_RANK), 0.01),
        'mla_kv_norm': 1.0 + nrm(ks[16], (N_ODD, C_KV_RANK), 0.01),
        'mla_w_uq': nrm(ks[17], (N_ODD, C_Q_RANK, C_HEADS * (C_NOPE + C_ROPE)), C_Q_RANK ** -0.5),
        'mla_w_ukv': nrm(ks[18], (N_ODD, C_KV_RANK, C_HEADS * (C_NOPE + C_V)), C_KV_RANK ** -0.5),
        'mla_w_out': nrm(ks[19], (N_ODD, C_HEADS * C_V, d), DEEPNORM_BETA * (C_HEADS * C_V) ** -0.5),
    }

def reference(x, c, positions, ada_w, ada_b, ln_g, ln_b, ffn_w_gate, ffn_w_up, ffn_w_down,
              hyb_w_in, hyb_w_out, attn_sink, hgrn_lb_logits, hgrn_norm_w,
              mla_w_down, mla_q_norm, mla_kv_norm, mla_w_uq, mla_w_ukv, mla_w_out):
    bsz = x.shape[0]
    cond = jax.nn.silu(c)
    lb_all = jnp.cumsum(jax.nn.softmax(hgrn_lb_logits.astype(F32), axis=0), axis=0)
    for layer in range(DEPTH):
        mod = (cond @ ada_w[layer] + ada_b[layer]).reshape(bsz, N_SUB, 3, D_MODEL)
        ffn_pre = lambda h, l=layer: swiglu(h, ffn_w_gate[l, 0], ffn_w_up[l, 0], ffn_w_down[l, 0])
        ffn_post = lambda h, l=layer: swiglu(h, ffn_w_gate[l, 1], ffn_w_up[l, 1], ffn_w_down[l, 1])
        if layer % 2 == 0:
            e = layer // 2
            mixer = lambda h, e=e, l=layer: hybrid_mixer(h, positions, hyb_w_in[e], hyb_w_out[e],
                                                         attn_sink[e], lb_all[l], hgrn_norm_w[e])
        else:
            o = layer // 2
            mixer = lambda h, o=o: mla(h, positions, mla_w_down[o], mla_q_norm[o], mla_kv_norm[o],
                                       mla_w_uq[o], mla_w_ukv[o], mla_w_out[o])
        x = modulated_sublayer(x, mod[:, 0], ln_g[layer, 0], ln_b[layer, 0], ffn_pre, 0.5)
        x = modulated_sublayer(x, mod[:, 1], ln_g[layer, 1], ln_b[layer, 1], mixer, 1.0)
        x = modulated_sublayer(x, mod[:, 2], ln_g[layer, 2], ln_b[layer, 2], ffn_post, 0.5)
    return x


_drawn_inputs = setup_inputs


def setup_inputs(seed=0):
    import zlib

    import numpy as np

    out = dict(_drawn_inputs(seed))
    spreads = {}
    factors = {'ada_b': 6.899,
     'attn_sink': 8.0,
     'hgrn_lb_logits': 8.0,
     'hgrn_norm_w': 8.0,
     'mla_q_norm': 8.0,
     'mla_kv_norm': 8.0}
    for name, (base, spread) in spreads.items():
        noise = np.random.default_rng([zlib.crc32(name.encode()), seed]).standard_normal(out[name].shape)
        drawn = base * np.exp(spread * noise) if base else spread * noise
        out[name] = jnp.asarray(drawn.astype(out[name].dtype))
    for name, factor in factors.items():
        out[name] = (out[name] * factor).astype(out[name].dtype)
    return out
```

```python
import math
from contextlib import ExitStack

import numpy as np

import concourse.bass as bass
from concourse import mybir

F32 = mybir.dt.float32
F32R = mybir.dt.float32r
I32 = mybir.dt.int32
ALU = mybir.AluOpType
ACT = mybir.ActivationFunctionType
AX = mybir.AxisListType

P = 128
D = 1024
SEQ = 256
DFF = 2816
KD = D // P
NT = SEQ // P
CW = 256
NCH = DFF // CW
DEPTH = 2
N_SUB = 3
ALPHA = (2 * DEPTH) ** 0.25
LN_EPS = 1e-5
RMS_EPS = 1e-6
TWO_PI = (6.28125, 0.001935005187988281, 3.019916033e-07)
RING = 6
RAW = 3
SLOT = 2048
ADA_RING = 4
ADA_W = 1024
PIECES = KD * 3


def build(nc, A, out):
    subs = [("ffn", 0, 0), ("hyb", 0, 0), ("ffn", 0, 1), ("ffn", 1, 0), ("mla", 1, 0), ("ffn", 1, 1)]
    last_sub = len(subs) - 1
    n_slots = {"ffn": 3 * NCH, "hyb": 17, "mla": 15}
    base = [0]
    for kind, _, _ in subs:
        base.append(base[-1] + n_slots[kind])
    ALL_SLOTS = base[-1]
    ffn_units = [2 * NCH * sum(k == "ffn" for k, _, _ in subs[:s]) for s in range(len(subs) + 1)]

    with ExitStack() as ctx:
        def sb(name, shape, dt=F32):
            return ctx.enter_context(nc.sbuf_tensor(name, shape, dt))

        def sem(name):
            return ctx.enter_context(nc.semaphore(name))

        w_raw = sb("w_raw", [P, RAW, SLOT])
        w_hi = sb("w_hi", [P, RING, SLOT], F32R)
        w_lo = sb("w_lo", [P, RING, SLOT], F32R)
        x = sb("x", [P, NT, D])
        hT_hi = sb("hT_hi", [P, KD, SEQ], F32R)
        hT_lo = sb("hT_lo", [P, KD, SEQ], F32R)
        gate_row = sb("gate_row", [P, 3, D])
        fT_hi = sb("fT_hi", [P, NT, CW], F32R)
        fT_lo = sb("fT_lo", [P, NT, CW], F32R)
        arena = sb("arena", [P, 11264])
        ident = sb("ident", [P, P])
        ones = sb("ones", [P, P])
        cond = sb("cond", [P, 2, KD])
        ln_nat = sb("ln_nat", [112, P])
        ln_col = sb("ln_col", [P, 112])
        mod_G = sb("mod_G", [P, 6, KD])
        mod_B = sb("mod_B", [P, 6, KD])
        mod_1s = sb("mod_1s", [P, KD])
        stats = sb("stats", [P, 2, 6])
        mean_var = sb("mean_var", [P, 2])
        var_eps = sb("var_eps", [P, 1])
        rstd = sb("rstd", [P, 1])
        neg_half = sb("neg_half", [P, 1])

        ada_raw = arena[:, 0:4096].rearrange("p (r n) -> p r n", r=ADA_RING)
        scratch = arena[:, 3072:4096]
        acc_gate0 = arena[:, 10240:11264]
        acc = arena[:, 4096:7168]
        sg = arena[:, 7168:7680].rearrange("p (t n) -> p t n", t=NT)
        hid = arena[:, 7680:8192].rearrange("p (t n) -> p t n", t=NT)
        ln_rows = arena[:, 8192:10240].rearrange("p (v n) -> p v n", v=2)

        spare_row = gate_row[:, 0, :]
        o_win = spare_row.rearrange("p (t n) -> p t n", t=NT)
        hf = arena[:, 0:2048].rearrange("p (d t n) -> p d t n", d=2, t=NT)
        hq = arena[:, 2048:3072].rearrange("p (t n) -> p t n", t=NT)
        hv = arena[:, 3072:4096].rearrange("p (t n) -> p t n", t=NT)
        tri = arena[:, 4096:4864].rearrange("p (d m n) -> p d m n", d=2, m=3)
        hg_gate = arena[:, 10240:11264].rearrange("p (t n) -> p t n", t=NT)
        k_dup = arena[:, 4864:5376].rearrange("p (t g n) -> p t g n", t=NT, g=2)
        qa = arena[:, 5376:6400].rearrange("p (t n) -> p t n", t=NT)
        win_s = arena[:, 4864:5892].rearrange("p (b a n) -> p b a n", b=2, a=2)
        va = arena[:, 6400:6656].rearrange("p (t n) -> p t n", t=NT)
        kT = arena[:, 6656:7168].rearrange("p (g n) -> p g n", g=2)
        qT = arena[:, 7168:8192].rearrange("p (h n) -> p h n", h=4)
        dist = arena[:, 8192:8704].rearrange("p (t n) -> p t n", t=NT)
        win_pT = arena[:, 8704:9728].rearrange("p (b n) -> p b n", b=2)
        norm_row = arena[:, 9728:10240]
        lb_rows = arena[:, 10240:11264].rearrange("p (v n) -> p v n", v=2)
        lb_logits = arena[:, 6656:8192].rearrange("p (v n) -> p v n", v=3)
        lb_tmp = arena[:, 8704:9216]
        pos_row = arena[:, 9216:9472].bitcast(I32)
        logf = arena[:, 4864:5376]
        hexp = arena[:, 5376:7424].rearrange("p (m n) -> p m n", m=4)
        hexpT = arena[:, 7424:8960].rearrange("p (m n) -> p m n", m=3)
        hA = arena[:, 8960:9216].rearrange("p (h n) -> p h n", h=4)
        hS = arena[:, 9216:10240].rearrange("p (d n) -> p d n", d=2)
        c_nat = arena[:, 0:1024].rearrange("p (t n) -> p t n", t=NT)
        c_tmp = arena[:, 1024:2048].rearrange("p (t n) -> p t n", t=NT)
        q_nat = arena[:, 2048:2816].rearrange("p (t h n) -> p t h n", t=NT, h=4)
        k_nat = arena[:, 4096:4864].rearrange("p (t h n) -> p t h n", t=NT, h=4)
        v_nat = arena[:, 0:1024].rearrange("p (b t n) -> p b t n", b=2, t=NT)
        mP = arena[:, 1024:2048].rearrange("p (b a n) -> p b a n", b=2, a=2)
        mpT = spare_row.rearrange("p (b n) -> p b n", b=2)
        mqT = arena[0:96, 4864:6912].rearrange("p (b h n) -> p b h n", b=2, h=4)
        mkT = arena[0:96, 6912:8960].rearrange("p (b h n) -> p b h n", b=2, h=4)
        m_o = arena[:, 8960:11008].rearrange("p (t n) -> p t n", t=NT)
        rp = arena[:, 2816:3072].rearrange("p (m h n) -> p m h n", m=4, h=4)
        kr_nat = sb("kr_nat", [P, NT, 32])
        norm_col = sb("norm_col", [P, 4])
        freq = sb("freq", [P, 16])
        angle = sb("angle", [P, 2, NT, 16])
        turns = arena[:, 1024:1088].rearrange("p (v t n) -> p v t n", v=2, t=NT)
        rot = sb("rot", [P, 2, NT, 16])

        pos_col = sb("pos_col", [P, NT], I32)
        sink_cols = sb("sink_cols", [P, 8])
        neg_max = sb("neg_max", [P, 2, 2])
        den = sb("den", [P, 4, 2])
        rden = sb("rden", [P, 4, 2])
        decay = sb("decay", [P, 8])
        half_sel = sb("half_sel", [P, 2])
        ssq = sb("ssq", [P, 8])
        rms = sb("rms", [P, 8])

        banks = [ctx.enter_context(nc.psum_tensor(f"bank{i}", [P, 512], F32)) for i in range(8)]
        Y = [[banks[0], banks[1]], [banks[2], banks[3]]]
        G = [banks[4], banks[5]]
        T = [banks[6], banks[7]]

        raw_full = [sem(f"raw_full{i}") for i in range(RAW)]
        hi_ready = sem("hi_ready")
        lo_ready = [sem(f"lo_ready{i}") for i in range(RING)]
        slot_used = sem("slot_used")
        ada_full = [sem(f"ada_full{i}") for i in range(ADA_RING)]
        acc_init = sem("acc_init")
        acc_bias = sem("acc_bias")
        acc_step = sem("acc_step")
        consts_in = sem("consts_in")
        cond_in = sem("cond_in")
        first_full = [sem(f"first_full{i}") for i in range(ADA_RING)]
        gate_bias = sem("gate_bias")
        x_in = [sem(f"x_in{t}") for t in range(NT)]
        ident_ready = sem("ident_ready")
        cond_ready = sem("cond_ready")
        ln_col_tr = sem("ln_col_tr")
        ln_col_ready = sem("ln_col_ready")
        ada_cols = sem("ada_cols")
        ada_gate = sem("ada_gate")
        mods_ready = sem("mods_ready")
        gate_ready = sem("gate_ready")
        gu_done = sem("gu_done")
        silu_done = sem("silu_done")
        hid_ready = sem("hid_ready")
        hid_tr = sem("hid_tr")
        fT_hi_ready = sem("fT_hi_ready")
        fT_ready = sem("fT_ready")
        y_ready = sem("y_ready")
        dve_step = sem("dve_step")
        var_ready = sem("var_ready")
        rstd_ready = sem("rstd_ready")
        n_ready = sem("n_ready")
        n_tr = sem("n_tr")
        hf_act = sem("hf_act")
        hf_dve = sem("hf_dve")
        h_hi_ready = sem("h_hi_ready")
        h_ready = sem("h_ready")
        pool_step = sem("pool_step")
        ln_rows_in = sem("ln_rows_in")
        x_ready = sem("x_ready")
        out_done = sem("out_done")
        mix_in = sem("mix_in")
        lb_exp = sem("lb_exp")
        lb_pre = sem("lb_pre")
        lb_done = sem("lb_done")
        diff_ready = sem("diff_ready")
        dist_abs = sem("dist_abs")
        dist_ready = sem("dist_ready")
        tri_ready = sem("tri_ready")
        proj_done = sem("proj_done")
        proj_read = sem("proj_read")
        qk_tr = sem("qk_tr")
        qk_act = sem("qk_act")
        qk_dve = sem("qk_dve")
        s_done = sem("s_done")
        s_max = sem("s_max")
        s_exp = sem("s_exp")
        p_tr = sem("p_tr")
        pT_ready = sem("pT_ready")
        pv_done = sem("pv_done")
        o_att = sem("o_att")
        f_ready = sem("f_ready")
        logf_ready = sem("logf_ready")
        k_ready = sem("k_ready")
        cum_done = sem("cum_done")
        hexp_ready = sem("hexp_ready")
        qe_ready = sem("qe_ready")
        ke_ready = sem("ke_ready")
        he_tr = sem("he_tr")
        heT_act = sem("heT_act")
        heT_dve = sem("heT_dve")
        hA_zero = sem("hA_zero")
        hA_done = sem("hA_done")
        hA_ready = sem("hA_ready")
        dS_done = sem("dS_done")
        S_ready = sem("S_ready")
        ho_done = sem("ho_done")
        sq_ready = sem("sq_ready")
        ms_ready = sem("ms_ready")
        rms_ready = sem("rms_ready")
        gate_mul = sem("gate_mul")
        ho_ready = sem("ho_ready")
        o_tr = sem("o_tr")
        o_hi = sem("o_hi")
        o_ready = sem("o_ready")
        mla_in = sem("mla_in")
        rden_ready = sem("rden_ready")
        freq_ready = sem("freq_ready")
        angle_ready = sem("angle_ready")
        rot_ready = sem("rot_ready")
        kr_done = sem("kr_done")
        q_rot = sem("q_rot")
        qk4_tr = sem("qk4_tr")
        qk4_ready = sem("qk4_ready")
        c_ready = sem("c_ready")
        c_tr = sem("c_tr")
        c_mul = sem("c_mul")
        c_hi = sem("c_hi")
        cT_ready = sem("cT_ready")

        ada = A["ada_w"].rearrange("l (p k) n -> l p k n", k=KD)

        ada_plan = {}
        for s, (kind, _, _) in enumerate(subs):
            if kind == "ffn":
                nxt = []
                n = s + 1
                while n <= last_sub:
                    nxt.append(n)
                    if subs[n][0] == "ffn":
                        break
                    n += 1
                ada_plan[s] = nxt

        def fin_of(s, c0):
            n = c0 // 5 - 1
            return ada_plan[s][n] if 0 <= n < len(ada_plan[s]) else None

        HG = [(512, 256), (0, 512), (1280, 512), (1792, 512), (768, 512), (2304, 512), (2816, 512)]
        HG_SLOT = [0, 1, 3, 5, 7, 9, 11]
        HOUT = 13

        def hybrid_plan():
            yield from (("enter", 0), ("proj", (0, 0)), ("enter", 1), ("proj", (0, 1)), ("proj", (1, 0)),
                        ("lb", 0), ("proj", (1, 1)), ("qk", 0))
            pieces = [(g, t) for g in range(2, 7) for t in range(NT)]
            for n, piece in enumerate(pieces):
                yield "proj", piece
                yield from attention_step(n, 8)
            yield "owin", 0
            yield "owin", 1
            yield "cum", 0
            for n in range(4):
                yield "turn", n
                if n < 3:
                    yield "cum", n + 1
                yield "chain", n
            yield "hnorm", 0
            yield "hnorm", 1
            yield from (("out", (0, 0)), ("out", (0, 1)), ("out", (1, 0)), ("out", (1, 1)), ("out", (2, 0)),
                        ("out", (3, 0)), ("out", (2, 1)), ("out", (3, 1)))

        M_SLOT = {"c": 0, "kr": 2, "uq": 3, "ukv": 4}
        MOUT = 11
        A0, P0, O0, R0 = 8, 14, 4, 2
        MLA_SCALE = 96 ** -0.5

        def mla_plan():
            yield from (("enter", 0), ("c", (0, 0)), ("enter", 1), ("c", (0, 1)), ("kr", (0, 0)), ("kr", (0, 1)),
                        ("cT", 0), ("cT", 1))

            def pieces(g):
                return [("uq", (g, 0)), ("uq", (g, 1)), ("ukv", (g, 0)), ("ukv", (g, 1))]
            yield from pieces(0)
            yield "qkT", 0
            for n in range(18):
                g = n // 4
                if g < 3:
                    yield pieces(g + 1)[n % 4]
                yield from attention_step(n, 16)
                if g < 3 and n % 4 == 3:
                    yield "qkT", g + 1
            yield "owin", 0
            yield "owin", 1
            yield from (("out", (0, 0)), ("out", (0, 1)), ("out", (1, 0)), ("out", (1, 1)), ("out", (2, 0)),
                        ("out", (3, 0)), ("out", (2, 1)), ("out", (3, 1)))

        def mla_piece(stage, m):
            g, t = m
            return {"c": 0, "kr": 2, "uq": 4 + 4 * g, "ukv": 6 + 4 * g}[stage] + t

        def mla_split(stage, m):
            g, t = m if isinstance(m, tuple) else (0, m)
            return {("c", 0): [2], ("c", 1): [3, 4], ("kr", 1): [5], ("cT", 0): [6], ("cT", 1): [7], ("uq", 1): [8 + 2 * g],
                    ("ukv", 1): [9 + 2 * g], ("owin", 0): [16]}.get((stage, t), [17] if (stage, m) == ("out", (0, 1)) else [])

        def mla_width(n):
            return 256 if n == 2 else (768, 1024)[(n + 1) % 2] if 3 <= n < MOUT else SLOT

        def slot_size(j):
            for s, (kind, _, _) in enumerate(subs):
                if kind == "mla" and base[s] <= j < base[s + 1]:
                    return mla_width(j - base[s])
            return SLOT

        def attention_step(n, units):
            for stage, m in (("S", n), ("P", n - 1), ("V", n - 2)):
                if 0 <= m < units:
                    yield stage, m

        def dS_index(m, jj):
            return 2 * m + jj if m < 2 else (4 + m - 2 if jj == 0 else None)

        def dS_before(m):
            return (0, 2, 4, 5)[m]

        def S_last(m, jj):
            return {(0, 1): 1, (1, 1): 3, (2, 0): 2, (3, 0): 4}[m, jj]

        HSTEP = [(0, 0), (1, 1), (0, 1), (1, 0)]

        FIRST = 2 * KD

        def first_piece(a):
            v, k = divmod(a, KD)
            return k, slice(v * D, (v + 1) * D), acc[:, v * D:(v + 1) * D] if v < 2 else acc_gate0

        def gate_base(s):
            return (2, 0)[s] if s < 2 else 2 * s

        class Count:
            def __init__(self, eng, s):
                self.eng, self.s, self.n = eng, s, 0

            def __call__(self, ins):
                ins.then_inc(self.s, 1)
                self.n += 1

            def wait(self):
                self.eng.wait_ge(self.s, self.n)

        def ffn_walk(eng, s, body):
            body(0, 0, None)
            for first, loop in ((1, 0), (6, 1)):
                with eng.Fori(0, 2) as i:
                    body(first, i, loop)
                    body(first + 1, i, loop)
                body(first + 4, 0, None)

        block = ctx.enter_context(nc.Block())

        @block.sync
        def _(sp):
            def load(j0, i, parts):
                if not (isinstance(i, int)) or j0 >= RAW:
                    j = j0 - RAW
                    sp.wait_ge(lo_ready[j % RING], j // RING + 1 + i)
                for dst, src in parts(w_raw[:, j0 % RAW, :]):
                    sp.dma_start(dst, src).then_inc(raw_full[j0 % RAW], 16)

            def block(w, rows, cols, width):
                def parts(raw):
                    k = (rows[1] - rows[0]) // P
                    v = raw[:, 0:k * width].rearrange("p (k n) -> p k n", k=k)
                    for h in range(2):
                        yield (v[:, h * k // 2:(h + 1) * k // 2, :],
                               w[rows[0] + h * k // 2 * P:rows[0] + (h + 1) * k // 2 * P, cols:cols + width]
                               .rearrange("(k p) n -> p k n", p=P))
                return parts

            def ffn_slot(l, half, kind, c):
                def parts(raw):
                    if kind < 2:
                        v = raw.rearrange("p (k n) -> p k n", k=4)
                        for n, w in enumerate((A["ffn_w_gate"], A["ffn_w_up"])):
                            yield (v[:, :, n * CW:(n + 1) * CW],
                                   w[l, half, kind * 512:kind * 512 + 512, bass.ds(c * CW, CW)]
                                   .rearrange("(k p) n -> p k n", p=P))
                    else:
                        for q in range(2):
                            yield (raw[:, q * D:(q + 1) * D],
                                   A["ffn_w_down"][l, half, bass.ds(c * CW + q * P, P), :])
                return parts

            sp.dma_start(cond[:, 0, :], A["c"][0].rearrange("(p k) -> p k", k=KD)).then_inc(cond_in, 16)
            for a in range(FIRST):
                if a >= ADA_RING:
                    sp.wait_ge(acc_step, a - ADA_RING + 1)
                k, cols, _ = first_piece(a)
                sp.dma_start(ada_raw[:, a % ADA_RING, :], ada[0, :, k, cols]).then_inc(first_full[a % ADA_RING], 16)
            for s, (kind, l, half) in enumerate(subs):
                if kind == "ffn":
                    def body(c0, i, loop):
                        for q in range(3):
                            load(base[s] + 3 * c0 + q, i, ffn_slot(l, half, q, c0 + 2 * i))
                    ffn_walk(sp, s, body)
                if kind == "mla":
                    with nc.allow_non_contiguous_dma(reason="few words"):
                        sp.wait_ge(diff_ready, 2)
                        sp.dma_start(pos_col[:, :], A["positions"][0].rearrange("(t p) -> p t", p=P)).then_inc(mla_in, 16)
                        for v, w in enumerate((A["mla_q_norm"], A["mla_kv_norm"])):
                            sp.dma_start(norm_col[:, 2 * v:2 * v + 2], w[0].rearrange("(k p) -> p k", p=P))\
                                .then_inc(mla_in, 16)
                    for n in range(2):
                        load(base[s] + n, 0, block(A["mla_w_down"][0], (n * 512, n * 512 + 512), 0, 512))
                    load(base[s] + 2, 0, block(A["mla_w_down"][0], (0, D), 512, 32))
                    for g in range(4):
                        load(base[s] + 3 + 2 * g, 0, block(A["mla_w_uq"][0], (0, 256), g * 384, 384))
                        load(base[s] + 4 + 2 * g, 0, block(A["mla_w_ukv"][0], (0, 256), g * 512, 512))
                    for n in range(4):
                        load(base[s] + MOUT + n, 0, block(A["mla_w_out"][0], (n * 256, n * 256 + 256), 0, D))
                if kind == "hyb":
                    win = A["hyb_w_in"][0]

                    def mixer_inputs():
                        sp.wait_ge(x_ready, 2 * s)
                        sp.dma_start(lb_logits, A["hgrn_lb_logits"].rearrange("(o a) n -> o a n", o=1)
                                     .broadcast_to([P, 3, 512])).then_inc(mix_in, 16)
                        sp.dma_start(pos_row, A["positions"].broadcast_to([P, SEQ])).then_inc(mix_in, 16)
                        with nc.allow_non_contiguous_dma(reason="256 words"):
                            sp.dma_start(pos_col[:, :], A["positions"][0].rearrange("(t p) -> p t", p=P))\
                                .then_inc(mix_in, 16)
                        sp.dma_start(sink_cols[:, :], A["attn_sink"].broadcast_to([P, 8])).then_inc(mix_in, 16)
                        sp.dma_start(norm_row, A["hgrn_norm_w"].rearrange("o h n -> o (h n)").broadcast_to([P, 512]))\
                            .then_inc(mix_in, 16)
                    for g, (c0, width) in enumerate(HG):
                        for n in range(width * KD // SLOT):
                            rows = (n * 512, n * 512 + 512) if width == 512 else (0, D)
                            load(base[s] + HG_SLOT[g] + n, 0, block(win, rows, c0, width))
                        if g == 2:
                            mixer_inputs()
                    for n in range(4):
                        load(base[s] + HOUT + n, 0, block(A["hyb_w_out"][0], (n * 256, n * 256 + 256), 0, D))
            for t in range(NT):
                sp.wait_ge(x_ready, 2 * last_sub + t + 1)
                sp.dma_start(out[0, t * P:(t + 1) * P, :], x[:, t, :]).then_inc(out_done, 16)
            sp.wait_ge(out_done, 32)

        @block.gpsimd
        def _(pool):
            step = Count(pool, pool_step)
            def ada_piece(s, n0, i):
                l, sub = divmod(s, N_SUB)
                a = s * PIECES + n0
                if a >= ADA_RING:
                    pool.wait_ge(acc_step, a - ADA_RING + 1 + 12 * i)
                k, v = divmod(n0, 3)
                pool.dma_start(ada_raw[:, a % ADA_RING, :],
                               ada[l, :, k + 4 * i, sub * 3 * D + v * D:sub * 3 * D + (v + 1) * D])\
                    .then_inc(ada_full[a % ADA_RING], 16)

            def acc_start(s):
                if s == 1:
                    pool.wait_ge(ada_cols, 1)
                else:
                    pool.wait_ge(ada_gate, gate_base(s))
                nc.gpsimd.memset(acc, 0.0).then_inc(acc_init, 1)
                pool.wait_ge(acc_init, s + 1)
                l, sub = divmod(s, N_SUB)
                pool.dma_start(acc[0:1, :], A["ada_b"][l:l + 1, sub * 3 * D:(sub + 1) * 3 * D])\
                    .then_inc(acc_bias, 16)

            step(nc.gpsimd.memset(ident[:, :], 0.0))
            step.wait()
            nc.gpsimd.affine_select(out=ident[:, :], in_=ident[:, :], compare_op=ALU.not_equal, fill=1.0,
                                    base=0, pattern=[[-1, P]], channel_multiplier=1).then_inc(ident_ready, 1)
            nc.gpsimd.memset(ones[:, :], 1.0).then_inc(ident_ready, 1)
            nc.gpsimd.memset(neg_half[:, :], -0.5).then_inc(ident_ready, 1)
            pool.wait_ge(ident_ready, 3)
            for v, w in enumerate((A["ln_g"], A["ln_b"])):
                pool.dma_start(ln_nat[48 * v:48 * v + 48, :],
                               w.rearrange("l s (j p) -> (l s j) p", p=P)).then_inc(consts_in, 16)
            pool.dma_start(ln_nat[96:112, :], A["ada_b"][0, 0:2 * D].rearrange("(j p) -> j p", p=P))\
                .then_inc(consts_in, 16)
            pool.dma_start(x[:, 1, :], A["x"][0, P:2 * P, :]).then_inc(x_in[1], 16)
            pool.wait_ge(h_ready, 2)
            for a in range(FIRST, PIECES):
                pool.wait_ge(acc_step, a - ADA_RING + 1)
                k, cols, _ = first_piece(a)
                pool.dma_start(ada_raw[:, a % ADA_RING, :], ada[0, :, k, cols]).then_inc(ada_full[a % ADA_RING], 16)

            def ln_tail(s):
                l, sub = divmod(s, N_SUB)
                if subs[s][0] == "hyb":
                    pool.wait_ge(ho_done, 8)
                elif subs[s][0] == "mla":
                    pool.wait_ge(o_ready, O0 + 4)
                for v, w in enumerate((A["ln_g"], A["ln_b"])):
                    pool.dma_start(ln_rows[:, v, :], w[l, sub:sub + 1, :].broadcast_to([P, D]))\
                        .then_inc(ln_rows_in, 16)
                for t in range(NT):
                    u = 2 * s + t
                    pool.wait_ge(var_ready, u + 1)
                    nc.gpsimd.tensor_tensor(rstd[:, :], var_eps[:, :], neg_half[:, :], ALU.pow).then_inc(rstd_ready, 1)
                    pool.wait_ge(n_ready, u + 1)
                    if s < last_sub:
                        pool.wait_ge(n_tr, 2 * (u + 3))
                    pool.wait_ge(ln_rows_in, 32 * (s + 1))
                    step(nc.gpsimd.tensor_tensor(x[:, t, :], x[:, t, :], ln_rows[:, 0, :], ALU.mult))
                    step.wait()
                    nc.gpsimd.tensor_tensor(x[:, t, :], x[:, t, :], ln_rows[:, 1, :], ALU.add).then_inc(x_ready, 1)
                pool.wait_ge(x_ready, 2 * (s + 1))

            for s, (kind, _, _) in enumerate(subs):
                if kind == "ffn":
                    for loop, nxt in enumerate(ada_plan[s]):
                        acc_start(nxt)
                        if loop == 0:
                            pool.wait_ge(h_ready, 2 * s + 2)
                        with pool.Fori(0, 2) as i:
                            for n in range(12):
                                ada_piece(nxt, n, i)
                if kind == "hyb":
                    pool.wait_ge(y_ready, 2 * s)
                    F, B = tri[:, 0, 0, :], tri[:, 1, 0, :]
                    step(nc.gpsimd.memset(tri[:, :, 0, :], 1.0))
                    step(nc.gpsimd.memset(half_sel[:, :], 0.0))
                    step.wait()
                    step(nc.gpsimd.affine_select(out=F, in_=F, compare_op=ALU.is_ge, fill=0.0, base=0,
                                                 pattern=[[1, P]], channel_multiplier=-1))
                    step(nc.gpsimd.affine_select(out=B, in_=B, compare_op=ALU.is_ge, fill=0.0, base=0,
                                                 pattern=[[-1, P]], channel_multiplier=1))
                    step.wait()
                    step(nc.gpsimd.memset(F[0:64, 64:128], 0.0))
                    step(nc.gpsimd.memset(B[64:128, 0:64], 0.0))
                    step(nc.gpsimd.memset(half_sel[0:64, 0:1], 1.0))
                    step(nc.gpsimd.memset(half_sel[64:128, 1:2], 1.0))
                    step.wait()
                    step(nc.gpsimd.tensor_copy(tri[:, 0, 1, :], F))
                    step(nc.gpsimd.tensor_copy(tri[:, 1, 1, :], B))
                    step(nc.gpsimd.tensor_tensor(tri[:, 0, 2, :], B, ident[:, :], ALU.subtract))
                    step(nc.gpsimd.tensor_tensor(tri[:, 1, 2, :], F, ident[:, :], ALU.subtract))
                    step.wait()
                    for j in range(2):
                        for d in range(2):
                            blk = tri[64 * j + 32 * d:64 * j + 32 * d + 32, d, 1, 64 * j:64 * j + 64]
                            step(nc.gpsimd.tensor_scalar(blk, blk, -1.0, None, ALU.add))
                    step.wait()
                    pool.sem_inc(tri_ready, 1)
                    pool.wait_ge(mix_in, 80)
                    for t in range(NT):
                        nc.gpsimd.tensor_tensor(dist[:, t, :].bitcast(I32), pos_row,
                                                pos_col[:, t:t + 1].broadcast_to([P, SEQ]), ALU.subtract)\
                            .then_inc(diff_ready, 1)
                    pool.wait_ge(dist_abs, 1)
                    for t in range(NT):
                        nc.gpsimd.affine_select(out=dist[:, t, :], in_=dist[:, t, :], compare_op=ALU.is_ge,
                                                fill=1e30, base=P if t == 0 else 0,
                                                pattern=[[-1 if t == 0 else 1, SEQ]],
                                                channel_multiplier=1 if t == 0 else -1).then_inc(dist_ready, 1)
                    pool.wait_ge(lb_done, 1)
                    for stage, m in hybrid_plan():
                        if stage == "proj" and m[0] in (2, 3):
                            (g, t), d = m, m[0] - 2
                            pool.wait_ge(proj_read, 2 * g + t + 1)
                            step(nc.gpsimd.tensor_tensor(hf[:, d, t, :], hf[:, d, t, :], lb_rows[:, 1, :], ALU.mult))
                            step.wait()
                            nc.gpsimd.tensor_tensor(hf[:, d, t, :], hf[:, d, t, :], lb_rows[:, 0, :], ALU.add)\
                                .then_inc(f_ready, 1)
                        elif stage == "proj" and m[0] == 6:
                            pool.wait_ge(proj_read, 2 * m[0] + m[1] + 1)
                            nc.gpsimd.tensor_tensor(hg_gate[:, m[1], :], hg_gate[:, m[1], :], norm_row, ALU.mult)\
                                .then_inc(gate_mul, 1)
                        elif stage == "cum":
                            d, t = HSTEP[m]
                            pool.wait_ge(logf_ready, m + 1)
                            nc.gpsimd.tensor_scalar(hf[:, d, t, :], hf[:, d, t, :], -1.0, 1.0, ALU.mult, ALU.add)\
                                .then_inc(k_ready, 1)
                        elif stage == "turn":
                            d, t = HSTEP[m]
                            if m == 0:
                                pool.wait_ge(o_att, 8)
                            if m > 0:
                                pool.wait_ge(ho_done, 2 * m)
                            nc.gpsimd.memset(hA[:, :, :], 0.0).then_inc(hA_zero, 1)
                            pool.wait_ge(k_ready, m + 1)
                            for n, e in ((2, 1), (4, 3)):
                                pool.wait_ge(hexp_ready, 5 * m + n)
                                nc.gpsimd.tensor_tensor(hexp[:, e, :], hexp[:, e, :], hf[:, d, t, :], ALU.mult)\
                                    .then_inc(ke_ready, 1)
                        elif stage == "hnorm":
                            pool.wait_ge(ms_ready, m + 1)
                            nc.gpsimd.tensor_tensor(rms[:, 4 * m:4 * m + 4], ssq[:, 4 * m:4 * m + 4],
                                                    neg_half[:, 0:1].broadcast_to([P, 4]), ALU.pow).then_inc(rms_ready, 1)
                if kind == "mla":
                    pool.wait_ge(y_ready, 2 * s)
                    for n in range(16):
                        op = nc.gpsimd.memset(freq[:, n:n + 1], float(np.float32(10000.0) ** np.float32(-n / 16)))
                    op.then_inc(freq_ready, 1)

                    def rotate(x, t, done, outs):
                        h = x.shape[1]
                        cos, sin = (rot[:, v, t:t + 1, :].broadcast_to([P, h, 16]) for v in range(2))
                        a, b = x[:, :, 0:16], x[:, :, 16:32]
                        for n, (u, v) in enumerate(((a, cos), (b, sin), (a, sin), (b, cos))):
                            step(nc.gpsimd.tensor_tensor(rp[:, n, 0:h, :], u, v, ALU.mult))
                        step.wait()
                        for out in outs:
                            nc.gpsimd.tensor_tensor(out[:, :, 0:16], rp[:, 0, 0:h, :], rp[:, 1, 0:h, :], ALU.subtract)
                            op = nc.gpsimd.tensor_tensor(out[:, :, 16:32], rp[:, 2, 0:h, :], rp[:, 3, 0:h, :], ALU.add)
                        op.then_inc(done, 1)

                    for stage, m in mla_plan():
                        if stage == "c":
                            t = m[1]
                            pool.wait_ge(ms_ready, R0 + t + 1)
                            nc.gpsimd.tensor_tensor(rms[:, 2 * t:2 * t + 2], ssq[:, 2 * t:2 * t + 2],
                                                    neg_half[:, 0:1].broadcast_to([P, 2]), ALU.pow).then_inc(rms_ready, 1)
                        elif stage == "kr":
                            t = m[1]
                            if t == 0:
                                pool.wait_ge(rot_ready, 1)
                            pool.wait_ge(proj_read, P0 + mla_piece(stage, m) + 1)
                            if t == 1:
                                pool.wait_ge(kr_done, 1)
                            rotate(kr_nat[:, t:t + 1, :], t, kr_done, [k_nat[:, t, h:h + 1, 64:96] for h in range(4)])
                        elif stage == "uq":
                            g, t = m
                            pool.wait_ge(proj_read, P0 + mla_piece(stage, m) + 1)
                            if g == 0 and t == 0:
                                pool.wait_ge(kr_done, 2)
                            else:
                                pool.wait_ge(q_rot, 2 * g + t)
                            x_rope = q_nat[:, t, :, 64:96]
                            rotate(x_rope, t, q_rot, [x_rope])
                ln_tail(s)

        @block.scalar
        def _(act):
            def split_hi(j0, i):
                if isinstance(i, int) and j0 >= ALL_SLOTS:
                    return
                act.wait_ge(raw_full[j0 % RAW], 32 * (j0 // RAW + 1 + RING // RAW * i))
                if j0 >= RING:
                    act.wait_ge(slot_used, j0 - RING + 1 + RING * i)
                n = slot_size(j0)
                nc.scalar.activation(w_hi[:, j0 % RING, 0:n], w_raw[:, j0 % RAW, 0:n], ACT.Copy).then_inc(hi_ready, 1)

            def enter(s, tiles):
                for t in tiles:
                    u = 2 * s + t
                    act.wait_ge(n_tr, 2 * u + 1)
                    if t == 0:
                        act.wait_ge(mods_ready, s + 1)
                    if u > 0:
                        act.wait_ge(h_ready, u)
                    for k in range(4):
                        mm = nc.scalar.activation(scratch[:, k * P:(k + 1) * P], G[t][:, k * P:(k + 1) * P],
                                                  ACT.Identity, bias=mod_B[:, s, k:k + 1], scale=mod_G[:, s, k:k + 1])
                    mm.then_inc(hf_act, 1)
                    act.wait_ge(hf_act, u + 1)
                    act.wait_ge(hf_dve, u + 1)
                    nc.scalar.activation(hT_hi[:, :, t * P:(t + 1) * P],
                                         scratch.rearrange("p (k n) -> p k n", k=KD), ACT.Copy).then_inc(h_hi_ready, 1)

            def attention_exp(m):
                act.wait_ge(s_max, m + 1)
                if m >= 4:
                    act.wait_ge(o_att, m - 3)
                for a in range(2):
                    op = nc.scalar.activation(win_s[:, m % 2, a, :], win_s[:, m % 2, a, :], ACT.Exp,
                                              bias=neg_max[:, m % 2, a:a + 1], accum_out=den[:, m % 4, a:a + 1])
                op.then_inc(s_exp, 1)

            def gate_half(s, half, bank):
                w = 0.5 if subs[s][0] == "ffn" else 1.0
                act.wait_ge(ada_gate, gate_base(s) + 2 - half)
                nc.scalar.activation(gate_row[:, s % 3, half * 512:half * 512 + 512], bank[:, :], ACT.Copy,
                                     bias=w, scale=w).then_inc(gate_ready, 1)

            act.dma_start(x[:, 0, :], A["x"][0, 0:P, :]).then_inc(x_in[0], 16)
            act.wait_ge(cond_in, 16)
            nc.scalar.activation(cond[:, 1, :], cond[:, 0, :], ACT.Silu).then_inc(cond_ready, 1)
            act.wait_ge(acc_init, 1)
            act.dma_start(acc_gate0[0:1, :], A["ada_b"][0:1, 2 * D:3 * D]).then_inc(gate_bias, 16)
            split_hi(0, 0)
            for s, (kind, _, _) in enumerate(subs):
                if kind == "ffn":
                    for t in range(NT):
                        enter(s, (t,))
                        if s == 0:
                            split_hi(t + 1, 0)
                    if s > 0 and subs[s - 1][0] == "ffn":
                        split_hi(base[s] + 2, 0)

                    def body(c0, i, loop):
                        u = ffn_units[s] + 2 * c0 + 4 * i
                        nxt = base[s] + 3 * (c0 + 1)
                        fin = None if loop is not None else fin_of(s, c0)
                        for t in range(NT):
                            act.wait_ge(gu_done, u + t + 1)
                            nc.scalar.activation(sg[:, t, :], G[t][:, 0:CW], ACT.Silu).then_inc(silu_done, 1)
                            if t == 1 and fin is not None:
                                gate_half(fin, 0, T[0])
                            if t == 0 or c0 < NCH - 1:
                                split_hi(nxt + 2 * t, i)
                            act.wait_ge(hid_tr, u + t + 1)
                            nc.scalar.activation(fT_hi[:, t, :], T[t][:, 0:CW], ACT.Copy).then_inc(fT_hi_ready, 1)
                            if t == 0:
                                if fin is not None:
                                    gate_half(fin, 1, G[0])
                                split_hi(nxt + 1, i)
                            elif fin == 1:
                                gate_half(0, 1, G[1])
                                gate_half(0, 0, G[1])
                    ffn_walk(act, s, body)
                if kind == "mla":
                    for stage, m in mla_plan():
                        if stage == "enter":
                            enter(s, (m,))
                            if m == 1:
                                act.wait_ge(angle_ready, 1)
                                nc.scalar.activation(rot[:, :, :, :], angle[:, :, :, :], ACT.Sin).then_inc(rot_ready, 1)
                        elif stage == "c":
                            t = m[1]
                            act.wait_ge(proj_done, P0 + t + 1)
                            nc.scalar.activation(c_tmp[:, t, :], banks[t][:, :], ACT.Square).then_inc(sq_ready, 1)
                        elif stage == "cT":
                            act.wait_ge(c_tr, m + 1)
                            for k in range(4):
                                op = nc.scalar.activation(c_tmp[:, m, k * P:(k + 1) * P], banks[6 + m][:, k * P:(k + 1) * P],
                                                          ACT.Copy, scale=norm_col[:, k:k + 1])
                            op.then_inc(c_mul, 1)
                            act.wait_ge(c_mul, m + 1)
                            nc.scalar.activation(hT_hi[:, 0:4, m * P:(m + 1) * P],
                                                 c_tmp[:, m, :].rearrange("p (k n) -> p k n", k=4), ACT.Copy)\
                                .then_inc(c_hi, 1)
                        elif stage == "uq":
                            g, t = m
                            act.wait_ge(proj_done, P0 + mla_piece(stage, m) + 1)
                            if g > 0:
                                act.wait_ge(qk4_tr, 2 * g)
                            nc.scalar.activation(q_nat[:, t, :, :], banks[t][:, 0:384].rearrange("p (h n) -> p h n", h=4),
                                                 ACT.Copy, scale=MLA_SCALE).then_inc(proj_read, 1)
                        elif stage == "ukv":
                            g, t = m
                            act.wait_ge(proj_done, P0 + mla_piece(stage, m) + 1)
                            kv = banks[t][:, :].rearrange("p (h n) -> p h n", h=4)
                            nc.scalar.activation(k_nat[:, t, :, 0:64], kv[:, :, 0:64], ACT.Copy)
                            nc.scalar.activation(v_nat[:, g % 2, t, :].rearrange("p (h n) -> p h n", h=4), kv[:, :, 64:128],
                                                 ACT.Copy).then_inc(proj_read, 1)
                        elif stage == "S":
                            b = m % 2
                            act.wait_ge(s_max, A0 + m + 1)
                            if m >= 2:
                                act.wait_ge(p_tr, A0 + m - 1)
                            if m >= 4:
                                act.wait_ge(o_att, A0 + m - 3)
                            if m == 0:
                                act.wait_ge(cT_ready, 2)
                            for a in range(2):
                                op = nc.scalar.activation(mP[:, b, a, :], banks[2 + b][:, a * SEQ:(a + 1) * SEQ], ACT.Exp,
                                                          bias=neg_max[:, b, a:a + 1], accum_out=den[:, m % 4, a:a + 1])
                            op.then_inc(s_exp, 1)
                        elif stage == "V":
                            g, t, p = m // 4, m % 4 // 2, m % 2
                            act.wait_ge(pv_done, A0 + m + 1)
                            act.wait_ge(rden_ready, m + 1)
                            for a in range(2):
                                h = 4 * g + 2 * p + a
                                op = nc.scalar.activation(m_o[:, t, h * 64:h * 64 + 64], banks[5][:, a * 64:a * 64 + 64],
                                                          ACT.Copy, scale=rden[:, m % 4, a:a + 1])
                            op.then_inc(o_att, 1)
                        elif stage == "owin":
                            for half in range(2):
                                bank = banks[(6, 7, 2, 3)[2 * m + half]]
                                act.wait_ge(o_tr, O0 + 2 * m + half + 1)
                                nc.scalar.activation(hT_hi[:, 4 * half:4 * half + 4, m * P:(m + 1) * P],
                                                     bank[:, :].rearrange("p (k n) -> p k n", k=4), ACT.Copy)\
                                    .then_inc(o_hi, 1)
                        for n in mla_split(stage, m):
                            split_hi(base[s] + n, 0)
                if kind == "hyb":
                    for stage, m in hybrid_plan():
                        if stage == "enter":
                            enter(s, (m,))
                            if m == 1:
                                split_hi(base[s] + 2, 0)
                        elif stage == "lb":
                            act.wait_ge(diff_ready, 2)
                            nc.scalar.activation(dist[:, :, :], dist[:, :, :].bitcast(I32), ACT.Abs).then_inc(dist_abs, 1)
                            act.wait_ge(lb_pre, 1)
                            nc.scalar.activation(lb_logits, lb_logits, ACT.Exp).then_inc(lb_exp, 1)
                        elif stage == "proj":
                            g, t = m
                            act.wait_ge(proj_done, 2 * g + t + 1)
                            b = Y[0][t]
                            if g == 0:
                                kk = b[:, 0:128].rearrange("p (g n) -> p g n", g=2)
                                for c in range(2):
                                    nc.scalar.activation(k_dup[:, t, :, c * 64:c * 64 + 64], kk, ACT.Copy)
                                op = nc.scalar.activation(va[:, t, :], b[:, 128:256], ACT.Copy)
                            elif g == 1:
                                op = nc.scalar.activation(qa[:, t, :], b[:, :], ACT.Copy, scale=0.125)
                            elif g in (2, 3):
                                op = nc.scalar.activation(hf[:, g - 2, t, :], b[:, :], ACT.Sigmoid)
                            elif g == 4:
                                op = nc.scalar.activation(hq[:, t, :], b[:, :], ACT.Silu)
                            elif g == 5:
                                op = nc.scalar.activation(hv[:, t, :], b[:, :], ACT.Copy)
                            else:
                                if t == 0:
                                    act.wait_ge(f_ready, 4)
                                op = nc.scalar.activation(hg_gate[:, t, :], b[:, :], ACT.Silu)
                            op.then_inc(proj_read, 1)
                            if 2 * g + t >= 1:
                                split_hi(base[s] + 2 * g + t + 2, 0)
                        elif stage == "qk":
                            act.wait_ge(lb_done, 1)
                            for n in range(2):
                                act.wait_ge(qk_tr, n + 1)
                                nc.scalar.activation(qT[:, 2 * n:2 * n + 2, :], G[n][:, :], ACT.Copy).then_inc(qk_act, 1)
                        elif stage == "S":
                            attention_exp(m)
                        elif stage == "P":
                            act.wait_ge(p_tr, m + 1)
                            if m >= 2:
                                act.wait_ge(pv_done, m - 1)
                            nc.scalar.activation(win_pT[:, m % 2, :], banks[6][:, :], ACT.Copy).then_inc(pT_ready, 1)
                        elif stage == "owin":
                            if m == 0:
                                for n in range(3):
                                    split_hi(base[s] + 16 + n, 0)
                            act.wait_ge(o_tr, m + 1)
                            nc.scalar.activation(hT_hi[:, 0:4, m * P:(m + 1) * P],
                                                 banks[m][:, :].rearrange("p (k n) -> p k n", k=4), ACT.Copy)\
                                .then_inc(o_hi, 1)
                        elif stage == "cum":
                            d, t = HSTEP[m]
                            act.wait_ge(f_ready, 4)
                            if m == 0:
                                act.wait_ge(o_att, 8)
                            if m > 0:
                                act.wait_ge(cum_done, 4 * m)
                            nc.scalar.activation(logf, hf[:, d, t, :], ACT.Ln).then_inc(logf_ready, 1)
                        elif stage == "turn":
                            for n, (e, src, scale) in enumerate(((0, 4, 1.0), (1, 4, -1.0), (2, 5, 1.0), (3, 6, 1.0))):
                                act.wait_ge(cum_done, 4 * m + (1, 1, 2, 3)[n])
                                if n == 0 and m > 0:
                                    act.wait_ge(he_tr, 3 * m)
                                if n == 3 and m > 0:
                                    act.wait_ge(dS_done, dS_before(m))
                                nc.scalar.activation(hexp[:, e, :], banks[src][:, :], ACT.Exp, scale=scale)\
                                    .then_inc(hexp_ready, 1)
                            act.wait_ge(cum_done, 4 * m + 4)
                            if m > 0:
                                act.wait_ge(S_ready, dS_before(m))
                            nc.scalar.activation(decay[:, :], banks[7][:, 0:8], ACT.Exp).then_inc(hexp_ready, 1)
                        elif stage == "hnorm":
                            if m == 0:
                                act.wait_ge(ho_done, 8)
                            nc.scalar.activation(hexp[:, m, :], banks[2 + m][:, :], ACT.Square).then_inc(sq_ready, 1)
                            act.wait_ge(o_tr, 2 + m + 1)
                            nc.scalar.activation(hT_hi[:, 4:8, m * P:(m + 1) * P],
                                                 banks[4 + m][:, :].rearrange("p (k n) -> p k n", k=4), ACT.Copy)\
                                .then_inc(o_hi, 1)
                        elif stage == "out" and m == (0, 1):
                            split_hi(base[s] + 19, 0)

        @block.vector
        def _(dve):
            step = Count(dve, dve_step)

            def split_lo(j0, i):
                if isinstance(i, int) and j0 >= ALL_SLOTS:
                    return
                dve.wait_ge(hi_ready, j0 + 1 + RING * i)
                n = slot_size(j0)
                nc.vector.tensor_tensor(w_lo[:, j0 % RING, 0:n], w_raw[:, j0 % RAW, 0:n],
                                        w_hi[:, j0 % RING, 0:n].bitcast(F32), ALU.subtract)\
                    .then_inc(lo_ready[j0 % RING], 1)

            def ada_piece(s, n0, i):
                a = s * PIECES + n0
                k, v = divmod(n0, 3)
                dve.wait_ge(ada_full[a % ADA_RING], 16 * ((a - FIRST) // ADA_RING + 1 + 3 * i))
                if n0 == 0:
                    dve.wait_ge(acc_bias, 16 * s)
                if a > 2:
                    dve.wait_ge(acc_step, a - 2 + 12 * i)
                nc.vector.scalar_tensor_tensor(out=acc[:, v * D:(v + 1) * D], in0=ada_raw[:, a % ADA_RING, :],
                                               scalar=cond[:, 1, bass.ds(k + 4 * i, 1)], in1=acc[:, v * D:(v + 1) * D],
                                               op0=ALU.mult, op1=ALU.add).then_inc(acc_step, 1)

            def enter(s, tiles):
                for t in tiles:
                    u = 2 * s + t
                    dve.wait_ge(n_tr, 2 * u + 2)
                    if u > 0:
                        dve.wait_ge(h_ready, u)
                    if t == 0:
                        dve.wait_ge(mods_ready, s + 1)
                    for k in range(4, 8):
                        op = nc.vector.tensor_scalar(scratch[:, k * P:(k + 1) * P], T[t][:, (k - 4) * P:(k - 3) * P],
                                                     mod_G[:, s, k:k + 1], mod_B[:, s, k:k + 1], ALU.mult, ALU.add)
                    op.then_inc(hf_dve, 1)
                    dve.wait_ge(h_hi_ready, u + 1)
                    nc.vector.tensor_tensor(hT_lo[:, :, t * P:(t + 1) * P],
                                            scratch.rearrange("p (k n) -> p k n", k=KD),
                                            hT_hi[:, :, t * P:(t + 1) * P].bitcast(F32), ALU.subtract)\
                        .then_inc(h_ready, 1)

            def mods(s, bank):
                dve.wait_ge(ada_cols, s + 1)
                if s == 0:
                    nc.vector.scalar_tensor_tensor(out=mod_G[:, 0, :], in0=bank[:, 8:16], scalar=1.0,
                                                   in1=ln_col[:, 104:112], op0=ALU.add, op1=ALU.add)
                    nc.vector.tensor_tensor(mod_B[:, 0, :], bank[:, 0:8], ln_col[:, 96:104], ALU.add)\
                        .then_inc(mods_ready, 1)
                    return
                step(nc.vector.tensor_scalar(mod_1s[:, :], bank[:, 8:16], 1.0, None, ALU.add))
                step.wait()
                g, b = ln_col[:, (s - 1) * 8:s * 8], ln_col[:, 48 + (s - 1) * 8:48 + s * 8]
                nc.vector.tensor_tensor(mod_G[:, s, :], mod_1s[:, :], g, ALU.mult)
                step(nc.vector.tensor_tensor(mod_B[:, s, :], mod_1s[:, :], b, ALU.mult))
                step.wait()
                nc.vector.tensor_tensor(mod_B[:, s, :], mod_B[:, s, :], bank[:, 0:8], ALU.add).then_inc(mods_ready, 1)

            def norm(s, t):
                u = 2 * s + t
                dve.wait_ge(y_ready, u + 1)
                if t == 0:
                    dve.wait_ge(gate_ready, max(gate_base(s) + 2, 4))
                if s > 0:
                    dve.wait_ge(x_ready, 2 * (s - 1) + t + 1)
                dve.wait_ge(h_ready, 2 * s + 2 + (t == 1 and s < last_sub))
                for half in range(2):
                    c = slice(half * 512, half * 512 + 512)
                    step(nc.vector.tensor_tensor(scratch[:, c], Y[t][half][:, :], gate_row[:, s % 3, c], ALU.mult))
                for half in range(2):
                    c = slice(half * 512, half * 512 + 512)
                    dve.wait_ge(dve_step, step.n - 1)
                    step(nc.vector.scalar_tensor_tensor(out=x[:, t, c], in0=x[:, t, c], scalar=ALPHA,
                                                        in1=scratch[:, c], op0=ALU.mult, op1=ALU.add))
                for half in range(2):
                    c = slice(half * 512, half * 512 + 512)
                    dve.wait_ge(dve_step, step.n - 1)
                    step(nc.vector.bn_stats(stats[:, half, :], x[:, t, c]))
                step.wait()
                step(nc.vector.bn_aggr(mean_var[:, :], stats[:, :, :]))
                step.wait()
                nc.vector.tensor_scalar(var_eps[:, :], mean_var[:, 1:2], LN_EPS, None, ALU.add).then_inc(var_ready, 1)
                dve.wait_ge(rstd_ready, u + 1)
                nc.vector.tensor_scalar(x[:, t, :], x[:, t, :], mean_var[:, 0:1], rstd[:, 0:1],
                                        ALU.subtract, ALU.mult).then_inc(n_ready, 1)

            def hybrid(s):
                for stage, m in hybrid_plan():
                    if stage == "enter":
                        if m == 1:
                            enter(s, (1,))
                            split_lo(base[s] + 2, 0)
                    elif stage == "lb":
                        dve.wait_ge(mix_in, 80)
                        step(nc.vector.tensor_tensor(lb_tmp, lb_logits[:, 0, :], lb_logits[:, 1, :], ALU.max))
                        step.wait()
                        step(nc.vector.tensor_tensor(lb_tmp, lb_tmp, lb_logits[:, 2, :], ALU.max))
                        step.wait()
                        for v in range(3):
                            op = nc.vector.tensor_tensor(lb_logits[:, v, :], lb_logits[:, v, :], lb_tmp, ALU.subtract)
                        op.then_inc(lb_pre, 1)
                        dve.wait_ge(lb_exp, 1)
                        step(nc.vector.tensor_tensor(lb_tmp, lb_logits[:, 0, :], lb_logits[:, 1, :], ALU.add))
                        step.wait()
                        step(nc.vector.tensor_tensor(lb_tmp, lb_tmp, lb_logits[:, 2, :], ALU.add))
                        step.wait()
                        step(nc.vector.reciprocal(lb_tmp, lb_tmp))
                        step.wait()
                        step(nc.vector.tensor_tensor(lb_rows[:, 0, :], lb_logits[:, 0, :], lb_tmp, ALU.mult))
                        step.wait()
                        nc.vector.tensor_scalar(lb_rows[:, 1, :], lb_rows[:, 0, :], -1.0, 1.0, ALU.mult, ALU.add)\
                            .then_inc(lb_done, 1)
                    elif stage == "proj":
                        if 2 * m[0] + m[1] >= 1:
                            split_lo(base[s] + 2 * m[0] + m[1] + 2, 0)
                    elif stage == "qk":
                        dve.wait_ge(qk_tr, 3)
                        nc.vector.tensor_copy(kT[:, :, :], banks[6][:, :].rearrange("p (g n) -> p g n", g=2))\
                            .then_inc(qk_dve, 1)
                        dve.wait_ge(dist_ready, 2)
                    elif stage == "S":
                        t, p = divmod(m, 4)
                        b = m % 2
                        dve.wait_ge(s_done, m + 1)
                        if m == 0:
                            dve.wait_ge(qk_act, 2)
                        if m >= 2:
                            dve.wait_ge(p_tr, m - 1)
                        for a in range(2):
                            h = 2 * p + a
                            nc.vector.scalar_tensor_tensor(out=win_s[:, b, a, 0:SEQ], in0=dist[:, t, :],
                                                           scalar=-2.0 ** -(h + 1),
                                                           in1=banks[2 + 2 * b + a][:, 0:SEQ],
                                                           op0=ALU.mult, op1=ALU.add)
                        step(nc.vector.tensor_copy(win_s[:, b, :, SEQ], sink_cols[:, 2 * p:2 * p + 2]))
                        step.wait()
                        nc.vector.tensor_reduce(neg_max[:, b, :], win_s[:, b, :, :], AX.X, ALU.max, negate=True)\
                            .then_inc(s_max, 1)
                    elif stage == "V":
                        t, p = divmod(m, 4)
                        b = m % 4
                        dve.wait_ge(s_exp, m + 1)
                        if m >= 4:
                            dve.wait_ge(o_att, m - 3)
                        step(nc.vector.reciprocal(rden[:, b, :], den[:, b, :]))
                        dve.wait_ge(pv_done, m + 1)
                        step.wait()
                        for a in range(2):
                            h = 2 * p + a
                            op = nc.vector.tensor_scalar(o_win[:, t, h * 64:h * 64 + 64],
                                                         banks[7][:, a * 64:a * 64 + 64], rden[:, b, a:a + 1],
                                                         None, ALU.mult)
                        op.then_inc(o_att, 1)
                    elif stage == "owin":
                        if m == 0:
                            for n in range(3):
                                split_lo(base[s] + 16 + n, 0)
                        out_lo(m, 0, banks[m], m)
                    elif stage == "turn":
                        for n, e in ((1, 0), (3, 2)):
                            dve.wait_ge(hexp_ready, 5 * m + n)
                            nc.vector.tensor_tensor(hexp[:, e, :], hexp[:, e, :], hq[:, HSTEP[m][1], :], ALU.mult)\
                                .then_inc(qe_ready, 1)
                        for n, b in ((0, 4), (1, 5), (2, 6)):
                            dve.wait_ge(he_tr, 3 * m + n + 1)
                            if n == 2 and m > 0:
                                dve.wait_ge(ho_done, 2 * m)
                            nc.vector.tensor_copy(hexpT[:, n, :], banks[b][:, :]).then_inc(heT_dve, 1)
                        dve.wait_ge(hA_done, m + 1)
                        dve.wait_ge(hA_zero, m + 1)
                        d = HSTEP[m][0]
                        for j in range(2):
                            rows = slice(64 * j, 64 * j + 64)
                            mask = tri[rows, d, 0, 64 * j:64 * j + 64].bitcast(I32)
                            for h in range(4):
                                op = nc.vector.copy_predicated(hA[rows, h, :], mask,
                                                               banks[0][rows, h * 64:h * 64 + 64])
                        op.then_inc(hA_ready, 1)
                    elif stage == "chain":
                        d, t = HSTEP[m]
                        for jj in range(2):
                            n = dS_index(m, jj)
                            if n is None:
                                continue
                            j = jj if d == 0 else 1 - jj
                            dve.wait_ge(dS_done, n + 1)
                            if jj == 0 and m < 2:
                                nc.vector.tensor_copy(hS[:, d, :], banks[1][:, :]).then_inc(S_ready, 1)
                                continue
                            dve.wait_ge(hexp_ready, 5 * (m + 1))
                            dve.wait_ge(S_ready, S_last(m, jj))
                            dve.wait_ge(ho_done, 2 * m + jj + 1)
                            for h in range(4):
                                c = slice(h * P, (h + 1) * P)
                                op = nc.vector.scalar_tensor_tensor(out=hS[:, d, c], in0=hS[:, d, c],
                                                                    scalar=decay[:, 2 * h + j:2 * h + j + 1],
                                                                    in1=banks[1][:, c], op0=ALU.mult, op1=ALU.add)
                            op.then_inc(S_ready, 1)
                    elif stage == "hnorm":
                        dve.wait_ge(sq_ready, m + 1)
                        step(nc.vector.tensor_reduce(ssq[:, 4 * m:4 * m + 4],
                                                     hexp[:, m, :].rearrange("p (h n) -> p h n", h=4), AX.X, ALU.add))
                        step.wait()
                        nc.vector.tensor_scalar(ssq[:, 4 * m:4 * m + 4], ssq[:, 4 * m:4 * m + 4], 1.0 / P, RMS_EPS,
                                                ALU.mult, ALU.add).then_inc(ms_ready, 1)
                        dve.wait_ge(rms_ready, m + 1)
                        dve.wait_ge(gate_mul, m + 1)
                        for h in range(4):
                            c = slice(h * P, (h + 1) * P)
                            op = nc.vector.scalar_tensor_tensor(out=hq[:, m, c], in0=banks[2 + m][:, c],
                                                                scalar=rms[:, 4 * m + h:4 * m + h + 1],
                                                                in1=hg_gate[:, m, c], op0=ALU.mult, op1=ALU.mult)
                        op.then_inc(ho_ready, 1)
                        out_lo(2 + m, 4, banks[4 + m], m)
                    elif stage == "out" and m == (0, 1):
                        split_lo(base[s] + 19, 0)

            def mla(s):
                for stage, m in mla_plan():
                    if stage == "enter":
                        if m == 1:
                            enter(s, (1,))
                            dve.wait_ge(mla_in, 48)
                            dve.wait_ge(freq_ready, 1)
                            for t in range(NT):
                                step(nc.vector.tensor_copy(turns[:, 0, t, 0:1], pos_col[:, t:t + 1]))
                            step.wait()
                            for t in range(NT):
                                for v in range(2):
                                    op = nc.vector.tensor_scalar(angle[:, v, t, :], freq[:, :], turns[:, 0, t, 0:1], None, ALU.mult)
                            step(op)
                            step.wait()
                            for v in range(2):
                                op = nc.vector.tensor_scalar(turns[:, v, :, :], angle[:, v, :, :], 0.5 / math.pi, (0.25, 0.0)[v],
                                                             ALU.mult, ALU.add)
                            step(op)
                            step.wait()
                            step(nc.vector.tensor_scalar(turns[:, :, :, :], turns[:, :, :, :], 12582912.0, -12582912.0,
                                                         ALU.add, ALU.add))
                            step.wait()
                            for part in TWO_PI:
                                step(nc.vector.scalar_tensor_tensor(out=angle[:, :, :, :], in0=turns[:, :, :, :], scalar=-part,
                                                                    in1=angle[:, :, :, :], op0=ALU.mult, op1=ALU.add))
                                step.wait()
                            step(nc.vector.tensor_scalar(angle[:, 0, :, :], angle[:, 0, :, :], math.pi / 2, None, ALU.add))
                            step.wait()
                            pi = float(np.float32(3.1415925))
                            nc.vector.tensor_scalar(angle[:, :, :, :], angle[:, :, :, :], pi, -pi, ALU.min, ALU.max)\
                                .then_inc(angle_ready, 1)
                    elif stage == "c":
                        t = m[1]
                        dve.wait_ge(sq_ready, R0 + t + 1)
                        c2 = slice(2 * t, 2 * t + 2)
                        step(nc.vector.tensor_reduce(ssq[:, c2], c_tmp[:, t, :].rearrange("p (v n) -> p v n", v=2),
                                                     AX.X, ALU.add))
                        step.wait()
                        nc.vector.tensor_scalar(ssq[:, c2], ssq[:, c2], 1.0 / 256, RMS_EPS, ALU.mult, ALU.add)\
                            .then_inc(ms_ready, 1)
                        dve.wait_ge(rms_ready, R0 + t + 1)
                        for v in range(2):
                            c = slice(v * 256, v * 256 + 256)
                            op = nc.vector.tensor_scalar(c_nat[:, t, c], banks[t][:, c], rms[:, 2 * t + v:2 * t + v + 1],
                                                         None, ALU.mult)
                        op.then_inc(proj_read, 1)
                    elif stage == "kr":
                        t = m[1]
                        dve.wait_ge(proj_done, P0 + 2 + t + 1)
                        nc.vector.tensor_copy(kr_nat[:, t, :], banks[2 + t][:, 0:32]).then_inc(proj_read, 1)
                    elif stage == "cT":
                        dve.wait_ge(c_hi, m + 1)
                        hi = hT_hi[:, 0:4, m * P:(m + 1) * P]
                        nc.vector.tensor_tensor(hT_lo[:, 0:4, m * P:(m + 1) * P],
                                                c_tmp[:, m, :].rearrange("p (k n) -> p k n", k=4), hi.bitcast(F32),
                                                ALU.subtract).then_inc(cT_ready, 1)
                    elif stage == "qkT":
                        for t in range(NT):
                            for n, dst in enumerate((mqT, mkT)):
                                bank = banks[(6, 7, 0, 1)[2 * t + n]]
                                dve.wait_ge(qk4_tr, 2 * m + t + 1)
                                nc.vector.tensor_copy(dst[:, m % 2, :, t * P:(t + 1) * P],
                                                      bank[0:96, :].rearrange("p (h n) -> p h n", h=4))\
                                    .then_inc(qk4_ready, 1)
                    elif stage == "S":
                        b = m % 2
                        dve.wait_ge(s_done, A0 + m + 1)
                        if m >= 2:
                            dve.wait_ge(s_exp, A0 + m - 1)
                        nc.vector.tensor_reduce(neg_max[:, b, :], banks[2 + b][:, :].rearrange("p (a n) -> p a n", a=2),
                                                AX.X, ALU.max, negate=True).then_inc(s_max, 1)
                    elif stage == "P":
                        dve.wait_ge(p_tr, A0 + m + 1)
                        if m >= 2:
                            dve.wait_ge(pv_done, A0 + m - 1)
                        nc.vector.tensor_copy(mpT[:, m % 2, :], banks[4][:, :]).then_inc(pT_ready, 1)
                        dve.wait_ge(s_exp, A0 + m + 1)
                        if m >= 4:
                            dve.wait_ge(o_att, A0 + m - 3)
                        nc.vector.reciprocal(rden[:, m % 4, :], den[:, m % 4, :]).then_inc(rden_ready, 1)
                    elif stage == "owin":
                        for half in range(2):
                            out_lo(O0 + 2 * m + half, 4 * half, banks[(6, 7, 2, 3)[2 * m + half]], m)
                    for n in mla_split(stage, m):
                        split_lo(base[s] + n, 0)

            def out_lo(n, k0, bank, t):
                dve.wait_ge(o_hi, n + 1)
                hi = hT_hi[:, k0:k0 + 4, t * P:(t + 1) * P]
                nc.vector.tensor_tensor(hT_lo[:, k0:k0 + 4, t * P:(t + 1) * P],
                                        bank[:, :].rearrange("p (k n) -> p k n", k=4), hi.bitcast(F32),
                                        ALU.subtract).then_inc(o_ready, 1)

            def first_step(a):
                k, _, part = first_piece(a)
                if a < FIRST:
                    dve.wait_ge(first_full[a % ADA_RING], 16 * (a // ADA_RING + 1))
                else:
                    dve.wait_ge(ada_full[a % ADA_RING], 16 * ((a - FIRST) // ADA_RING + 1))
                if a > 0:
                    dve.wait_ge(acc_step, a)
                if k == 0 and a < FIRST:
                    nc.vector.tensor_scalar(part, ada_raw[:, a % ADA_RING, :], cond[:, 1, 0:1], None, ALU.mult)\
                        .then_inc(acc_step, 1)
                    return
                nc.vector.scalar_tensor_tensor(out=part, in0=ada_raw[:, a % ADA_RING, :], scalar=cond[:, 1, k:k + 1],
                                               in1=part, op0=ALU.mult, op1=ALU.add).then_inc(acc_step, 1)

            nc.vector.memset(acc_gate0, 0.0).then_inc(acc_init, 1)
            dve.wait_ge(cond_ready, 1)
            for a in range(FIRST):
                first_step(a)
            dve.wait_ge(gate_bias, 16)
            dve.wait_ge(ln_col_tr, 1)
            nc.vector.tensor_copy(ln_col[:, :], G[1][:, 0:112]).then_inc(ln_col_ready, 1)
            dve.wait_ge(ln_col_ready, 1)
            mods(0, T[1])
            split_lo(0, 0)
            enter(0, (0,))
            split_lo(1, 0)
            for s, (kind, _, _) in enumerate(subs):
                if kind == "ffn":
                    enter(s, (1,))
                    if s == 0 or subs[s - 1][0] == "ffn":
                        split_lo(base[s] + 2, 0)
                    plan = ada_plan[s]

                    def body(c0, i, loop):
                        u = ffn_units[s] + 2 * c0 + 4 * i
                        nxt = base[s] + 3 * (c0 + 1)
                        for t in range(NT):
                            dve.wait_ge(silu_done, u + t + 1)
                            nc.vector.tensor_tensor(hid[:, t, :], sg[:, t, :], G[t][:, CW:2 * CW], ALU.mult)\
                                .then_inc(hid_ready, 1)
                            if loop is not None and loop < len(plan):
                                for n in range((0, 2)[t], (2, 4)[t]):
                                    ada_piece(plan[loop], 6 * ((c0 - 1) % 5) + n, i)
                            if t == 0 or c0 < NCH - 1:
                                split_lo(nxt + 2 * t, i)
                            dve.wait_ge(fT_hi_ready, u + t + 1)
                            nc.vector.tensor_tensor(fT_lo[:, t, :], T[t][:, 0:CW], fT_hi[:, t, :].bitcast(F32),
                                                    ALU.subtract).then_inc(fT_ready, 1)
                            if s == 0 and c0 == 0:
                                for a in range(FIRST, FIRST + 2) if t == 0 else range(FIRST + 2, PIECES):
                                    first_step(a)
                            if t == 0:
                                split_lo(nxt + 1, i)
                                if loop is None and fin_of(s, c0) is not None:
                                    mods(fin_of(s, c0), T[1])
                            if loop is not None and loop < len(plan) and t == 1:
                                for n in range(4, 6):
                                    ada_piece(plan[loop], 6 * ((c0 - 1) % 5) + n, i)
                    ffn_walk(dve, s, body)
                if kind == "hyb":
                    hybrid(s)
                if kind == "mla":
                    mla(s)
                norm(s, 0)
                if s < last_sub:
                    enter(s + 1, (0,))
                norm(s, 1)

        @block.tensor
        def _(pe):
            def ada_cols_of(s, bank):
                for v in range(2):
                    pe.wait_ge(acc_step, (s + 1) * PIECES if s > 0 else (v + 1) * KD)
                    for k in range(KD):
                        mm = nc.tensor.matmul(bank[:, v * KD + k:v * KD + k + 1],
                                              acc[:, v * D + k * P:v * D + (k + 1) * P], ones[:, 0:1],
                                              start=True, stop=True)
                mm.then_inc(ada_cols, 1)

            def ada_gate_of(s, half, bank):
                part = (acc_gate0 if s == 0 else acc[:, 2 * D:3 * D])[:, half * 512:half * 512 + 512]
                mm = nc.tensor.matmul(bank[:, :], ones[:, :], part,
                                      start=True, stop=True)
                mm.then_inc(ada_gate, 1)

            def enter(s, t):
                if s > 0:
                    pe.wait_ge(n_ready, 2 * (s - 1) + t + 1)
                for k in range(KD):
                    bank = (G, T)[k // 4][t]
                    mm = nc.tensor.transpose(bank[:, (k % 4) * P:(k % 4 + 1) * P], x[:, t, k * P:(k + 1) * P],
                                             ident[:, :])
                    if k % 4 == 3:
                        mm.then_inc(n_tr, 1)

            def product(dst, a_hi, a_lo, b_hi, b_lo, start, stop, before=None):
                mm = nc.tensor.matmul(dst, a_hi, b_hi, start=start, stop=False)
                if before is not None:
                    mm.then_inc(before, 1)
                nc.tensor.matmul(dst, a_lo, b_hi, start=False, stop=False)
                return nc.tensor.matmul(dst, a_hi, b_lo, start=False, stop=stop)

            def slot_wait(j0, i):
                pe.wait_ge(lo_ready[j0 % RING], j0 // RING + 1 + i)

            def out_project(s, n, t, slots, inputs):
                j0 = base[s] + slots + n
                if n == 0:
                    pe.wait_ge(o_ready, inputs)
                if t == 0:
                    slot_wait(j0, 0)
                for q in range(2):
                    for half in range(2):
                        k, w = 2 * n + q, slice(q * D + half * 512, q * D + half * 512 + 512)
                        tok = slice(t * P, (t + 1) * P)
                        mm = product(Y[t][half][:, :], hT_hi[:, k, tok], hT_lo[:, k, tok], w_hi[:, j0 % RING, w],
                                     w_lo[:, j0 % RING, w], k == 0, k == KD - 1)
                if n == 3:
                    mm.then_inc(y_ready, 1)
                    if t == 1:
                        pe.wait_ge(y_ready, 2 * s + 2)
                        pe.sem_inc(slot_used, 1)
                elif t == 1:
                    mm.then_inc(slot_used, 1)

            def mla(s):
                for stage, m in mla_plan():
                    if stage == "enter":
                        enter(s, m)
                    elif stage in M_SLOT:
                        g, t = m
                        piece = mla_piece(stage, m)
                        width, tiles = {"c": (512, KD), "kr": (32, KD), "uq": (384, 2), "ukv": (512, 2)}[stage]
                        k0 = 2 if stage == "ukv" else 0
                        bank = banks[t + (2 if stage == "kr" else 0)]
                        if stage == "c":
                            pe.wait_ge(h_ready, 2 * s + t + 1)
                        elif stage == "uq":
                            if g == 0:
                                pe.wait_ge(cT_ready, t + 1)
                            else:
                                pe.wait_ge(qk4_ready, 4 * g)
                            pe.wait_ge(proj_read, P0 + piece - (0 if g == 0 else 1))
                        elif stage == "ukv":
                            pe.wait_ge(proj_read, P0 + piece - 1)
                        per = min(tiles, SLOT // width)
                        for k in range(tiles):
                            j0 = base[s] + M_SLOT[stage] + 2 * g + k // per
                            if t == 0 and k % per == 0:
                                slot_wait(j0, 0)
                            w = slice(k % per * width, (k % per + 1) * width)
                            tok = slice(t * P, (t + 1) * P)
                            mm = product(bank[:, 0:width], hT_hi[:, k0 + k, tok], hT_lo[:, k0 + k, tok],
                                         w_hi[:, j0 % RING, w], w_lo[:, j0 % RING, w], k == 0, k == tiles - 1)
                            if t == 1 and k % per == per - 1 and k < tiles - 1:
                                mm.then_inc(slot_used, 1)
                        mm.then_inc(proj_done, 1)
                        if t == 1:
                            pe.wait_ge(proj_done, P0 + piece + 1)
                            pe.sem_inc(slot_used, 1)
                    elif stage == "cT":
                        pe.wait_ge(proj_read, P0 + 4)
                        for k in range(4):
                            mm = nc.tensor.transpose(banks[6 + m][:, k * P:(k + 1) * P], c_nat[:, m, k * P:(k + 1) * P],
                                                     ident[:, :])
                        mm.then_inc(c_tr, 1)
                    elif stage == "qkT":
                        pe.wait_ge(q_rot, 2 * m + 2)
                        pe.wait_ge(kr_done, 2)
                        pe.wait_ge(proj_read, P0 + mla_piece("ukv", (m, 1)) + 1)
                        for t in range(NT):
                            if t == 0 and m > 0:
                                pe.wait_ge(qk4_ready, 4 * m)
                            for n, src in enumerate((q_nat, k_nat)):
                                bank = banks[(6, 7, 0, 1)[2 * t + n]]
                                for h in range(4):
                                    mm = nc.tensor.transpose(bank[0:96, h * P:(h + 1) * P], src[:, t, h, :], ident[:, :])
                            mm.then_inc(qk4_tr, 1)
                    elif stage == "S":
                        g, t, p = m // 4, m % 4 // 2, m % 2
                        if m % 4 == 0:
                            pe.wait_ge(qk4_ready, 4 * g + 4)
                        if m >= 2:
                            pe.wait_ge(s_exp, A0 + m - 1)
                        for a in range(2):
                            h = 2 * p + a
                            mm = nc.tensor.matmul(banks[2 + m % 2][:, a * SEQ:(a + 1) * SEQ],
                                                  mqT[:, g % 2, h, t * P:(t + 1) * P], mkT[:, g % 2, h, :],
                                                  start=True, stop=True)
                        mm.then_inc(s_done, 1)
                    elif stage == "P":
                        pe.wait_ge(s_exp, A0 + m + 1)
                        if m > 0:
                            pe.wait_ge(pT_ready, A0 + m)
                        for a in range(2):
                            for kt in range(NT):
                                c = (2 * a + kt) * P
                                mm = nc.tensor.transpose(banks[4][:, c:c + P], mP[:, m % 2, a, kt * P:(kt + 1) * P],
                                                         ident[:, :])
                        mm.then_inc(p_tr, 1)
                    elif stage == "V":
                        g, t, p = m // 4, m % 4 // 2, m % 2
                        pe.wait_ge(pT_ready, A0 + m + 1)
                        if m > 0:
                            pe.wait_ge(o_att, A0 + m)
                        for a in range(2):
                            h = 2 * p + a
                            for kt in range(NT):
                                c = (2 * a + kt) * P
                                mm = nc.tensor.matmul(banks[5][:, a * 64:a * 64 + 64], mpT[:, m % 2, c:c + P],
                                                      v_nat[:, g % 2, kt, h * 64:h * 64 + 64],
                                                      start=kt == 0, stop=kt == 1)
                        mm.then_inc(pv_done, 1)
                    elif stage == "owin":
                        pe.wait_ge(o_att, A0 + 16)
                        for half in range(2):
                            for k in range(4):
                                c = (4 * half + k) * P
                                mm = nc.tensor.transpose(banks[(6, 7, 2, 3)[2 * m + half]][:, k * P:(k + 1) * P],
                                                         m_o[:, m, c:c + P], ident[:, :])
                            mm.then_inc(o_tr, 1)
                    elif stage == "out":
                        out_project(s, *m, MOUT, O0 + 4)

            def hybrid(s):
                for stage, m in hybrid_plan():
                    if stage == "enter":
                        enter(s, m)
                    elif stage == "proj":
                        g, t = m
                        width = HG[g][1]
                        if g == 0:
                            pe.wait_ge(h_ready, 2 * s + t + 1)
                        else:
                            pe.wait_ge(proj_read, 2 * g + t - 1)
                        per = SLOT // width
                        for k in range(KD):
                            j0 = base[s] + HG_SLOT[g] + k // per
                            if t == 0 and k % per == 0:
                                slot_wait(j0, 0)
                            w = slice(k % per * width, (k % per + 1) * width)
                            tok = slice(t * P, (t + 1) * P)
                            mm = product(Y[0][t][:, 0:width], hT_hi[:, k, tok], hT_lo[:, k, tok],
                                         w_hi[:, j0 % RING, w], w_lo[:, j0 % RING, w], k == 0, k == KD - 1)
                            if t == 1 and k % per == per - 1 and k < KD - 1:
                                mm.then_inc(slot_used, 1)
                        mm.then_inc(proj_done, 1)
                        if t == 1:
                            pe.wait_ge(proj_done, 2 * g + 2)
                            pe.sem_inc(slot_used, 1)
                    elif stage == "qk":
                        pe.wait_ge(proj_read, 4)
                        for n in range(2):
                            for q in range(2):
                                for t in range(NT):
                                    p = 2 * n + q
                                    mm = nc.tensor.transpose(G[n][:, q * SEQ + t * P:q * SEQ + (t + 1) * P],
                                                             qa[:, t, p * P:(p + 1) * P], ident[:, :])
                            mm.then_inc(qk_tr, 1)
                        for g in range(2):
                            for t in range(NT):
                                mm = nc.tensor.transpose(banks[6][:, g * SEQ + t * P:g * SEQ + (t + 1) * P],
                                                         k_dup[:, t, g, :], ident[:, :])
                        mm.then_inc(qk_tr, 1)
                    elif stage == "S":
                        t, p = divmod(m, 4)
                        if m == 0:
                            pe.wait_ge(qk_act, 2)
                            pe.wait_ge(qk_dve, 1)
                        if m >= 2:
                            pe.wait_ge(s_max, m - 1)
                        for a in range(2):
                            r = slice(64 * a, 64 * a + 64)
                            mm = nc.tensor.matmul(banks[2 + m % 2 * 2 + a][:, 0:SEQ],
                                                  qT[r, p, t * P:(t + 1) * P], kT[r, p // 2, :], start=True, stop=True)
                        mm.then_inc(s_done, 1)
                    elif stage == "P":
                        pe.wait_ge(s_exp, m + 1)
                        if m > 0:
                            pe.wait_ge(pT_ready, m)
                        for a in range(2):
                            for kt in range(NT):
                                c = (2 * a + kt) * P
                                mm = nc.tensor.transpose(banks[6][:, c:c + P], win_s[:, m % 2, a, kt * P:(kt + 1) * P],
                                                         ident[:, :])
                        mm.then_inc(p_tr, 1)
                    elif stage == "V":
                        t, p = divmod(m, 4)
                        pe.wait_ge(pT_ready, m + 1)
                        if m > 0:
                            pe.wait_ge(o_att, m)
                        for a in range(2):
                            for kt in range(NT):
                                c = (2 * a + kt) * P
                                mm = nc.tensor.matmul(banks[7][:, a * 64:a * 64 + 64], win_pT[:, m % 2, c:c + P],
                                                      va[:, kt, p // 2 * 64:p // 2 * 64 + 64],
                                                      start=kt == 0, stop=kt == 1)
                        mm.then_inc(pv_done, 1)
                    elif stage == "owin":
                        pe.wait_ge(o_att, 8)
                        pe.wait_ge(proj_read, 14)
                        for k in range(4):
                            mm = nc.tensor.transpose(banks[m][:, k * P:(k + 1) * P], o_win[:, m, k * P:(k + 1) * P],
                                                     ident[:, :])
                        mm.then_inc(o_tr, 1)
                    elif stage == "cum":
                        d, t = HSTEP[m]
                        pe.wait_ge(logf_ready, m + 1)
                        pe.wait_ge(tri_ready, 1)
                        for n, (mat, b) in enumerate(((1, 4), (0, 5), (2, 6))):
                            if m > 0:
                                pe.wait_ge(heT_dve, 3 * m - 2 + n)
                            nc.tensor.matmul(banks[b][:, :], tri[:, d, mat, :], logf, start=True, stop=True)\
                                .then_inc(cum_done, 1)
                        if m > 0:
                            pe.wait_ge(hexp_ready, 5 * m)
                        for h in range(4):
                            mm = nc.tensor.matmul(banks[7][:, 2 * h:2 * h + 2], logf[:, h * P:(h + 1) * P],
                                                  half_sel[:, :], start=True, stop=True)
                        mm.then_inc(cum_done, 1)
                    elif stage == "turn":
                        for n, e in enumerate((0, 1, 2)):
                            pe.wait_ge((qe_ready, ke_ready, qe_ready)[n], (2 * m + 1, 2 * m + 1, 2 * m + 2)[n])
                            pe.wait_ge(hexp_ready, 5 * m + 2 + n)
                            for h in range(4):
                                mm = nc.tensor.transpose(banks[4 + n][:, h * P:(h + 1) * P],
                                                         hexp[:, e, h * P:(h + 1) * P], ident[:, :])
                            mm.then_inc(he_tr, 1)
                        pe.wait_ge(heT_dve, 3 * m + 3)
                        if m == 0:
                            pe.wait_ge(o_ready, 2)
                        else:
                            pe.wait_ge(hA_ready, m)
                        for j in range(2):
                            for h in range(4):
                                c = slice(h * P + 64 * j, h * P + 64 * j + 64)
                                mm = nc.tensor.matmul(banks[0][64 * j:64 * j + 64, h * 64:h * 64 + 64],
                                                      hexpT[:, 1, c], hexpT[:, 0, c], start=True, stop=True)
                        mm.then_inc(hA_done, 1)
                    elif stage == "chain":
                        d, t = HSTEP[m]
                        pe.wait_ge(hA_ready, m + 1)
                        pe.wait_ge(ke_ready, 2 * m + 2)
                        for jj in range(2):
                            j = jj if d == 0 else 1 - jj
                            rows = slice(64 * j, 64 * j + 64)
                            first = m < 2 and jj == 0
                            if dS_index(m, jj) is not None:
                                if dS_index(m, jj) > 0:
                                    pe.wait_ge(S_ready, dS_index(m, jj))
                                for h in range(4):
                                    c = slice(h * P, (h + 1) * P)
                                    mm = nc.tensor.matmul(banks[1][:, c], hexp[rows, 3, c], hv[rows, t, c],
                                                          start=True, stop=True)
                                mm.then_inc(dS_done, 1)
                            if not first:
                                pe.wait_ge(S_ready, {(0, 1): 1, (1, 1): 3, (2, 0): 2, (3, 0): 4, (2, 1): 5, (3, 1): 6}[m, jj])
                            for h in range(4):
                                c = slice(h * P, (h + 1) * P)
                                o = banks[2 + t][rows, c]
                                mm = nc.tensor.matmul(o, hA[rows, h, :], hv[rows, t, c], start=m < 2 and h == 0,
                                                      stop=False, skip_group_check=True)
                                if not first:
                                    mm = nc.tensor.matmul(o, hexpT[:, 2, h * P + 64 * j:h * P + 64 * j + 64],
                                                          hS[:, d, c], start=False, stop=False, skip_group_check=True)
                            mm.then_inc(ho_done, 1)
                    elif stage == "hnorm":
                        pe.wait_ge(ho_ready, m + 1)
                        for k in range(4):
                            mm = nc.tensor.transpose(banks[4 + m][:, k * P:(k + 1) * P], hq[:, m, k * P:(k + 1) * P],
                                                     ident[:, :])
                        mm.then_inc(o_tr, 1)
                    elif stage == "out":
                        out_project(s, *m, HOUT, 4)

            pe.wait_ge(ident_ready, 3)
            pe.wait_ge(consts_in, 48)
            nc.tensor.transpose(G[1][:, 0:112], ln_nat[:, :], ident[0:112, 0:112]).then_inc(ln_col_tr, 1)
            pe.wait_ge(x_in[0], 16)
            enter(0, 0)
            ada_cols_of(0, T[1])
            pe.wait_ge(mods_ready, 1)
            pe.wait_ge(ln_col_ready, 1)
            pe.wait_ge(x_in[1], 16)
            enter(0, 1)

            for s, (kind, _, _) in enumerate(subs):
                if kind == "ffn":
                    plan = ada_plan[s]

                    def up(t, c0, i, ks):
                        u = ffn_units[s] + 2 * c0 + 4 * i + t
                        for k in ks:
                            j0 = base[s] + 3 * c0 + k // 4
                            if k == 0:
                                if c0 == 0 and isinstance(i, int):
                                    pe.wait_ge(h_ready, 2 * s + t + 1)
                                else:
                                    pe.wait_ge(hid_ready, u - 1)
                            if k % 4 == 0 and t == 0:
                                slot_wait(j0, i)
                            w = slice((k % 4) * 512, (k % 4 + 1) * 512)
                            tok = slice(t * P, (t + 1) * P)
                            mm = product(G[t][:, :], hT_hi[:, k, tok], hT_lo[:, k, tok],
                                         w_hi[:, j0 % RING, w], w_lo[:, j0 % RING, w], k == 0, k == KD - 1)
                            if k == 3 and t == 1:
                                mm.then_inc(slot_used, 1)
                        if ks[-1] == KD - 1:
                            mm.then_inc(gu_done, 1)

                    def turn(t, c0, i, frees_slot=False):
                        pe.wait_ge(hid_ready, ffn_units[s] + 2 * c0 + 4 * i + t + 1)
                        for q in range(2):
                            mm = nc.tensor.transpose(T[t][:, q * P:(q + 1) * P], hid[:, t, q * P:(q + 1) * P],
                                                     ident[:, :])
                            if q == 0 and frees_slot:
                                mm.then_inc(slot_used, 1)
                        mm.then_inc(hid_tr, 1)

                    def down(t, c0, i, frees_slot=False):
                        j0 = base[s] + 3 * c0 + 2
                        pe.wait_ge(fT_ready, ffn_units[s] + 2 * c0 + 4 * i + t + 1)
                        if t == 0:
                            slot_wait(j0, i)
                        for half in range(2):
                            for q in range(2):
                                w = slice(q * D + half * 512, q * D + half * 512 + 512)
                                mm = product(Y[t][half][:, :], fT_hi[:, t, q * P:(q + 1) * P],
                                             fT_lo[:, t, q * P:(q + 1) * P], w_hi[:, j0 % RING, w],
                                             w_lo[:, j0 % RING, w], c0 == 0 and q == 0, c0 == NCH - 1 and q == 1,
                                             slot_used if frees_slot and half == 0 and q == 0 else None)
                        if c0 == NCH - 1:
                            mm.then_inc(y_ready, 1)
                            if t == 1:
                                pe.wait_ge(y_ready, 2 * s + 2)
                                pe.sem_inc(slot_used, 1)
                        elif t == 1:
                            mm.then_inc(slot_used, 1)

                    def body(c0, i, loop):
                        fin = None if loop is not None else fin_of(s, c0)
                        if fin is not None:
                            ada_cols_of(fin, T[1])
                        turn(0, c0, i)
                        if fin is not None:
                            ada_gate_of(fin, 1, G[0])
                        if c0 < NCH - 1:
                            up(1, c0, i, range(KD))
                            down(0, c0, i, frees_slot=True)
                            if fin is not None:
                                ada_gate_of(fin, 0, T[0])
                                pe.wait_ge(mods_ready, fin + 1)
                            turn(1, c0, i)
                            if fin is not None:
                                pe.wait_ge(gate_ready, gate_base(fin) + 2)
                            if fin == 1:
                                ada_gate_of(0, 1, G[1])
                            up(0, c0 + 1, i, range(KD))
                            if fin == 1:
                                pe.wait_ge(gate_ready, 3)
                                ada_gate_of(0, 0, G[1])
                            down(1, c0, i)
                            if fin == 1:
                                pe.wait_ge(gate_ready, 4)
                        else:
                            up(1, c0, i, range(4))
                            down(0, c0, i)
                            if fin is not None:
                                ada_gate_of(fin, 0, T[0])
                                pe.wait_ge(mods_ready, fin + 1)
                            up(1, c0, i, range(4, KD))
                            turn(1, c0, i, frees_slot=True)
                            down(1, c0, i)
                            if fin is not None:
                                pe.wait_ge(gate_ready, gate_base(fin) + 2)

                    if s > 0:
                        enter(s, 0)
                    up(0, 0, 0, range(KD))
                    if s > 0:
                        enter(s, 1)
                    ffn_walk(pe, s, body)
                if kind == "hyb":
                    hybrid(s)
                if kind == "mla":
                    mla(s)


_INS = ["x", "c", "positions", "ada_w", "ada_b", "ln_g", "ln_b", "ffn_w_gate", "ffn_w_up", "ffn_w_down",
        "hyb_w_in", "hyb_w_out", "attn_sink", "hgrn_lb_logits", "hgrn_norm_w", "mla_w_down", "mla_q_norm",
        "mla_kv_norm", "mla_w_uq", "mla_w_ukv", "mla_w_out"]


def kernel(**inputs):
    import numpy as _np
    import concourse.bacc as _bacc
    from concourse import mybir as _mybir
    from concourse.bass_utils import run_bass_kernel_spmd as _run

    nc = _bacc.Bacc("TRN2", target_bir_lowering=False, num_devices=1)
    arrays, aps = {}, {}
    for name in _INS:
        a = _np.ascontiguousarray(inputs[name])
        arrays[f"in_{name}_dram"] = a
        aps[name] = nc.dram_tensor(f"in_{name}_dram", a.shape, _mybir.dt.from_np(a.dtype), kind="ExternalInput").ap()
    out = nc.dram_tensor("out_0_dram", (1, SEQ, D), F32, kind="ExternalOutput").ap()
    build(nc, aps, out)
    r = _run(nc, [arrays], core_ids=[0])
    return r.results[0]["out_0_dram"]
```

```python
import math
from contextlib import ExitStack

import numpy as np

import concourse.bass as bass
from concourse import mybir

F32 = mybir.dt.float32
F32R = mybir.dt.float32r
I32 = mybir.dt.int32
ALU = mybir.AluOpType
ACT = mybir.ActivationFunctionType
AX = mybir.AxisListType

P = 128
D = 1024
SEQ = 256
DFF = 2816
KD = D // P
NT = SEQ // P
CW = 256
NCH = DFF // CW
DEPTH = 2
N_SUB = 3
ALPHA = (2 * DEPTH) ** 0.25
LN_EPS = 1e-5
RMS_EPS = 1e-6
TWO_PI = (6.28125, 0.001935005187988281, 3.019916033e-07)
RING = 6
RAW = 3
SLOT = 2048
ADA_RING = 4
PIECES = KD * 3


def build(nc, A, out):
    subs = [("ffn", 0, 0), ("hyb", 0, 0), ("ffn", 0, 1), ("ffn", 1, 0), ("mla", 1, 0), ("ffn", 1, 1)]
    last_sub = len(subs) - 1
    n_slots = {"ffn": 3 * NCH, "hyb": 17, "mla": 15}
    base = [0]
    for kind, _, _ in subs:
        base.append(base[-1] + n_slots[kind])
    ALL_SLOTS = base[-1]
    ffn_units = [2 * NCH * sum(k == "ffn" for k, _, _ in subs[:s]) for s in range(len(subs) + 1)]

    with ExitStack() as ctx:
        def sb(name, shape, dt=F32):
            return ctx.enter_context(nc.sbuf_tensor(name, shape, dt))

        def sem(name):
            return ctx.enter_context(nc.semaphore(name))

        w_raw = sb("w_raw", [P, RAW, SLOT])
        w_hi = sb("w_hi", [P, RING, SLOT], F32R)
        w_lo = sb("w_lo", [P, RING, SLOT], F32R)
        x = sb("x", [P, NT, D])
        hT_hi = sb("hT_hi", [P, KD, SEQ], F32R)
        hT_lo = sb("hT_lo", [P, KD, SEQ], F32R)
        gate_row = sb("gate_row", [P, 3, D])
        fT_hi = sb("fT_hi", [P, NT, CW], F32R)
        fT_lo = sb("fT_lo", [P, NT, CW], F32R)
        arena = sb("arena", [P, 11264])
        ident = sb("ident", [P, P])
        ones = sb("ones", [P, P])
        cond = sb("cond", [P, 2, KD])
        ln_nat = sb("ln_nat", [112, P])
        ln_col = sb("ln_col", [P, 112])
        mod_G = sb("mod_G", [P, 6, KD])
        mod_B = sb("mod_B", [P, 6, KD])
        mod_1s = sb("mod_1s", [P, KD])
        stats = sb("stats", [P, 2, 6])
        mean_var = sb("mean_var", [P, 2])
        var_eps = sb("var_eps", [P, 1])
        rstd = sb("rstd", [P, 1])
        neg_half = sb("neg_half", [P, 1])

        ada_raw = arena[:, 0:4096].rearrange("p (r n) -> p r n", r=ADA_RING)
        scratch = arena[:, 3072:4096]
        acc_gate0 = arena[:, 10240:11264]
        acc = arena[:, 4096:7168]
        sg = arena[:, 7168:7680].rearrange("p (t n) -> p t n", t=NT)
        hid = arena[:, 7680:8192].rearrange("p (t n) -> p t n", t=NT)
        ln_rows = arena[:, 8192:10240].rearrange("p (v n) -> p v n", v=2)

        spare_row = gate_row[:, 0, :]
        o_win = spare_row.rearrange("p (t n) -> p t n", t=NT)
        hf = arena[:, 0:2048].rearrange("p (d t n) -> p d t n", d=2, t=NT)
        hq = arena[:, 2048:3072].rearrange("p (t n) -> p t n", t=NT)
        hv = arena[:, 3072:4096].rearrange("p (t n) -> p t n", t=NT)
        tri = arena[:, 4096:4864].rearrange("p (d m n) -> p d m n", d=2, m=3)
        hg_gate = arena[:, 10240:11264].rearrange("p (t n) -> p t n", t=NT)
        k_dup = arena[:, 4864:5376].rearrange("p (t g n) -> p t g n", t=NT, g=2)
        qa = arena[:, 5376:6400].rearrange("p (t n) -> p t n", t=NT)
        win_s = arena[:, 4864:5892].rearrange("p (b a n) -> p b a n", b=2, a=2)
        va = arena[:, 6400:6656].rearrange("p (t n) -> p t n", t=NT)
        kT = arena[:, 6656:7168].rearrange("p (g n) -> p g n", g=2)
        qT = arena[:, 7168:8192].rearrange("p (h n) -> p h n", h=4)
        dist = arena[:, 8192:8704].rearrange("p (t n) -> p t n", t=NT)
        win_pT = arena[:, 8704:9728].rearrange("p (b n) -> p b n", b=2)
        norm_row = arena[:, 9728:10240]
        lb_rows = arena[:, 10240:11264].rearrange("p (v n) -> p v n", v=2)
        lb_logits = arena[:, 1536:3072].rearrange("p (v n) -> p v n", v=3)
        lb_tmp = arena[:, 3072:3584]
        pos_row = arena[:, 9216:9472].bitcast(I32)
        logf = (arena[:, 4864:5376], arena[:, 9728:10240],
                spare_row[:, 0:512], spare_row[:, 512:1024])
        hexp = arena[:, 5376:7424].rearrange("p (m n) -> p m n", m=4)
        hexpT = arena[:, 7424:8960].rearrange("p (m n) -> p m n", m=3)
        hA = arena[:, 8960:9216].rearrange("p (h n) -> p h n", h=4)
        hS = arena[:, 9216:10240].rearrange("p (d n) -> p d n", d=2)
        c_nat = arena[:, 0:1024].rearrange("p (t n) -> p t n", t=NT)
        c_tmp = arena[:, 1024:2048].rearrange("p (t n) -> p t n", t=NT)
        q_nat = arena[:, 2048:2816].rearrange("p (t h n) -> p t h n", t=NT, h=4)
        k_nat = arena[:, 4096:4864].rearrange("p (t h n) -> p t h n", t=NT, h=4)
        v_nat = arena[:, 0:1024].rearrange("p (b t n) -> p b t n", b=2, t=NT)
        mP = arena[:, 1024:2048].rearrange("p (b a n) -> p b a n", b=2, a=2)
        mpT = spare_row.rearrange("p (b n) -> p b n", b=2)
        mqT = arena[0:96, 4864:6912].rearrange("p (b h n) -> p b h n", b=2, h=4)
        mkT = arena[0:96, 6912:8960].rearrange("p (b h n) -> p b h n", b=2, h=4)
        m_o = arena[:, 8960:11008].rearrange("p (t n) -> p t n", t=NT)
        rp = arena[:, 2816:3072].rearrange("p (m h n) -> p m h n", m=4, h=4)
        kr_nat = sb("kr_nat", [P, NT, 32])
        norm_col = sb("norm_col", [P, 4])
        freq = sb("freq", [P, 16])
        angle = sb("angle", [P, 2, NT, 16])
        turns = arena[:, 1024:1088].rearrange("p (v t n) -> p v t n", v=2, t=NT)
        rot = sb("rot", [P, 2, NT, 16])

        pos_col = sb("pos_col", [P, NT], I32)
        sink_cols = sb("sink_cols", [P, 8])
        neg_max = sb("neg_max", [P, 2, 2])
        den = sb("den", [P, 4, 2])
        rden = sb("rden", [P, 4, 2])
        decay = sb("decay", [P, 8])
        half_sel = sb("half_sel", [P, 2])
        ssq = sb("ssq", [P, 8])
        rms = sb("rms", [P, 8])

        banks = [ctx.enter_context(nc.psum_tensor(f"bank{i}", [P, 512], F32)) for i in range(8)]
        Y = [[banks[0], banks[1]], [banks[2], banks[3]]]
        G = [banks[4], banks[5]]
        T = [banks[6], banks[7]]

        raw_full = [sem(f"raw_full{i}") for i in range(RAW)]
        hi_ready = sem("hi_ready")
        lo_ready = [sem(f"lo_ready{i}") for i in range(RING)]
        slot_used = sem("slot_used")
        ada_full = [sem(f"ada_full{i}") for i in range(ADA_RING)]
        acc_init = sem("acc_init")
        acc_bias = sem("acc_bias")
        acc_step = sem("acc_step")
        consts_in = sem("consts_in")
        cond_in = sem("cond_in")
        first_full = [sem(f"first_full{i}") for i in range(ADA_RING)]
        gate_bias = sem("gate_bias")
        x_in = [sem(f"x_in{t}") for t in range(NT)]
        ident_ready = sem("ident_ready")
        cond_ready = sem("cond_ready")
        ln_col_tr = sem("ln_col_tr")
        ln_col_ready = sem("ln_col_ready")
        ada_cols = sem("ada_cols")
        ada_gate = sem("ada_gate")
        mods_ready = sem("mods_ready")
        gate_ready = sem("gate_ready")
        gu_done = sem("gu_done")
        silu_done = sem("silu_done")
        hid_ready = sem("hid_ready")
        hid_tr = sem("hid_tr")
        fT_hi_ready = sem("fT_hi_ready")
        fT_ready = sem("fT_ready")
        y_ready = sem("y_ready")
        dve_step = sem("dve_step")
        var_ready = sem("var_ready")
        rstd_ready = sem("rstd_ready")
        n_ready = sem("n_ready")
        n_tr = sem("n_tr")
        hf_act = sem("hf_act")
        hf_dve = sem("hf_dve")
        h_hi_ready = sem("h_hi_ready")
        h_ready = sem("h_ready")
        pool_step = sem("pool_step")
        ln_rows_in = sem("ln_rows_in")
        x_ready = sem("x_ready")
        out_done = sem("out_done")
        mix_in = sem("mix_in")
        lb_exp = sem("lb_exp")
        lb_max = sem("lb_max")
        lb_pre = sem("lb_pre")
        lb_sum = sem("lb_sum")
        lb_rows_ready = sem("lb_rows_ready")
        lb_rec = sem("lb_rec")
        diff_ready = sem("diff_ready")
        dist_abs = sem("dist_abs")
        dist_ready = sem("dist_ready")
        tri_ready = sem("tri_ready")
        proj_done = sem("proj_done")
        proj_read = sem("proj_read")
        qk_tr = sem("qk_tr")
        qk_act = sem("qk_act")
        qk_dve = sem("qk_dve")
        s_done = sem("s_done")
        s_max = sem("s_max")
        s_exp = sem("s_exp")
        p_tr = sem("p_tr")
        pT_ready = sem("pT_ready")
        pv_done = sem("pv_done")
        o_att = sem("o_att")
        sig_ready = sem("sig_ready")
        f_ready = sem("f_ready")
        hq_ready = sem("hq_ready")
        logf_ready = sem("logf_ready")
        k_ready = sem("k_ready")
        cum_done = sem("cum_done")
        hexp_ready = sem("hexp_ready")
        qe_ready = sem("qe_ready")
        ke_ready = sem("ke_ready")
        he_tr = sem("he_tr")
        heT_dve = sem("heT_dve")
        hA_zero = sem("hA_zero")
        hA_done = sem("hA_done")
        hA_ready = sem("hA_ready")
        dS_done = sem("dS_done")
        S_ready = sem("S_ready")
        ho_done = sem("ho_done")
        sq_ready = sem("sq_ready")
        ms_ready = sem("ms_ready")
        rms_ready = sem("rms_ready")
        gate_mul = sem("gate_mul")
        ho_ready = sem("ho_ready")
        o_tr = sem("o_tr")
        o_hi = sem("o_hi")
        o_ready = sem("o_ready")
        mla_in = sem("mla_in")
        rden_ready = sem("rden_ready")
        freq_ready = sem("freq_ready")
        angle_ready = sem("angle_ready")
        rot_ready = sem("rot_ready")
        kr_done = sem("kr_done")
        q_rot = sem("q_rot")
        qk4_tr = sem("qk4_tr")
        qk4_ready = sem("qk4_ready")
        c_tr = sem("c_tr")
        c_mul = sem("c_mul")
        c_hi = sem("c_hi")
        cT_ready = sem("cT_ready")

        ada = A["ada_w"].rearrange("l (p k) n -> l p k n", k=KD)

        ada_plan = {}
        for s, (kind, _, _) in enumerate(subs):
            if kind == "ffn":
                nxt = []
                n = s + 1
                while n <= last_sub:
                    nxt.append(n)
                    if subs[n][0] == "ffn":
                        break
                    n += 1
                ada_plan[s] = nxt

        def fin_of(s, c0):
            n = c0 // 5 - 1
            return ada_plan[s][n] if 0 <= n < len(ada_plan[s]) else None

        HG = [(512, 256), (0, 512), (1280, 512), (1792, 512), (768, 512), (2304, 512), (2816, 512)]
        HG_SLOT = [0, 1, 3, 5, 7, 9, 11]
        HOUT = 13

        def hybrid_plan():
            yield from (("enter", 0), ("proj", (0, 0)), ("enter", 1), ("proj", (0, 1)), ("split", (0, 1)),
                        ("proj", (1, 0)), ("split", (1, 0)), ("dist", 0), ("proj", (1, 1)), ("split", (1, 1)), ("qk", 0))
            pieces = [(g, t) for g in range(2, 7) for t in range(NT)]
            for n, piece in enumerate(pieces):
                yield "proj", piece
                yield from attention_step(n, 8)
                yield "split", piece
                yield from {0: (("lb", 0),), 1: (("lb", 1),), 4: (("sig", 0),)}.get(n, ())
            yield "owin", 0
            yield "owin", 1
            yield "log", 0
            yield from (("cum", 0), ("prod", 0), ("turn", 0))
            for n in range(4):
                if n < 3:
                    yield from (("cum", n + 1), ("prod", n + 1))
                yield "chain", n
                if n < 3:
                    yield "turn", n + 1
            yield from (("out", (0, 0)), ("out", (1, 0)), ("hnorm", 0), ("hnorm", 1), ("out", (0, 1)),
                        ("out", (1, 1)), ("out", (2, 0)), ("out", (3, 0)), ("out", (2, 1)), ("out", (3, 1)))

        M_SLOT = {"c": 0, "kr": 2, "uq": 3, "ukv": 4}
        MOUT = 11
        A0, P0, O0, R0 = 8, 14, 4, 2
        MLA_SCALE = 96 ** -0.5

        def mla_plan():
            yield from (("enter", 0), ("c", (0, 0)), ("enter", 1), ("c", (0, 1)), ("cn", 0), ("cn", 1),
                        ("kr", (0, 0)), ("kr", (0, 1)), ("cT", 0), ("cT", 1))
            yield from (("uq", (0, 0)), ("uq", (0, 1)), ("ukv", (0, 0)), ("ukv", (0, 1)), ("qkT", (0, 0)),
                        ("qkT", (0, 1)))
            for n in range(18):
                g, q = divmod(n, 4)
                if g < 3:
                    yield from ((("uq", (g + 1, 0)),), (("uq", (g + 1, 1)),), (("ukv", (g + 1, 0)),),
                                (("qkT", (g + 1, 0)), ("ukv", (g + 1, 1))))[q]
                yield from {13: (("out", (0, 0)),), 14: (("out", (1, 0)),), 16: (("owin", (0, 1)),),
                            17: (("out", (2, 0)),)}.get(n, ())
                yield from attention_step(n, 16)
                if g < 3 and q == 3:
                    yield "qkT", (g + 1, 1)
                yield from {12: (("owin", (0, 0)),), 14: (("owin", (1, 0)),)}.get(n, ())
            yield from (("owin", (1, 1)), ("out", (3, 0)), ("out", (0, 1)), ("out", (1, 1)), ("out", (2, 1)),
                        ("out", (3, 1)))

        def mla_piece(stage, m):
            g, t = m
            return {"c": 0, "kr": 2, "uq": 4 + 4 * g, "ukv": 6 + 4 * g}[stage] + t

        def mla_bank(stage, t):
            return banks[t + 2 if stage == "kr" else t]

        def mla_split(stage, m):
            if stage == "owin":
                return [16] if m == (0, 0) else []
            if stage == "out":
                return [17] if m == (0, 1) else []
            g, t = m if isinstance(m, tuple) else (0, m)
            return {("cn", 0): [3], ("cn", 1): [4], ("kr", 1): [5], ("cT", 0): [6], ("cT", 1): [7], ("ukv", 0): [8 + 2 * g],
                    ("qkT", 1): [9 + 2 * g]}.get((stage, t), [])

        def mla_width(n):
            return 256 if n == 2 else (768, 1024)[(n + 1) % 2] if 3 <= n < MOUT else SLOT

        def slot_size(j):
            for s, (kind, _, _) in enumerate(subs):
                if kind == "mla" and base[s] <= j < base[s + 1]:
                    return mla_width(j - base[s])
            return SLOT

        def attention_step(n, units):
            for stage, m in (("S", n), ("P", n - 1), ("V", n - 2)):
                if 0 <= m < units:
                    yield stage, m

        def dS_index(m, jj):
            return 2 * m + jj if m < 2 else (4 + m - 2 if jj == 0 else None)

        def dS_before(m):
            return (0, 2, 4, 5)[m]

        def S_last(m, jj):
            return {(0, 1): 1, (1, 1): 3, (2, 0): 2, (3, 0): 4}[m, jj]

        HSTEP = [(0, 0), (1, 1), (0, 1), (1, 0)]

        FIRST = 2 * KD
        GATE0 = FIRST + PIECES

        def ada_base(s):
            return FIRST if s == 1 else s * PIECES

        def first_piece(a):
            v, k = divmod(a, KD)
            return k, slice(v * D, (v + 1) * D), acc[:, v * D:(v + 1) * D] if v < 2 else acc_gate0

        def gate_base(s):
            return (2, 0)[s] if s < 2 else 2 * s

        class Count:
            def __init__(self, eng, s):
                self.eng, self.s, self.n = eng, s, 0

            def __call__(self, ins):
                ins.then_inc(self.s, 1)
                self.n += 1

            def wait(self):
                self.eng.wait_ge(self.s, self.n)

        def entry_banks(s, t):
            return Y[t] if subs[s][0] == "ffn" else (G[t], T[t])

        def turned(k):
            n = k // 4 * 2 + k % 2
            return slice(n * P, (n + 1) * P)

        def ffn_walk(eng, s, body):
            body(0, 0, None)
            for first, loop in ((1, 0), (6, 1)):
                with eng.Fori(0, 2) as i:
                    body(first, i, loop)
                    body(first + 1, i, loop)
                body(first + 4, 0, None)

        block = ctx.enter_context(nc.Block())

        @block.sync
        def _(sp):
            def load(j0, i, parts):
                if not (isinstance(i, int)) or j0 >= RAW:
                    j = j0 - RAW
                    sp.wait_ge(lo_ready[j % RING], j // RING + 1 + i)
                for dst, src in parts(w_raw[:, j0 % RAW, :]):
                    sp.dma_start(dst, src).then_inc(raw_full[j0 % RAW], 16)

            def block(w, rows, cols, width):
                def parts(raw):
                    k = (rows[1] - rows[0]) // P
                    v = raw[:, 0:k * width].rearrange("p (k n) -> p k n", k=k)
                    for h in range(2):
                        yield (v[:, h * k // 2:(h + 1) * k // 2, :],
                               w[rows[0] + h * k // 2 * P:rows[0] + (h + 1) * k // 2 * P, cols:cols + width]
                               .rearrange("(k p) n -> p k n", p=P))
                return parts

            def ffn_slot(l, half, kind, c):
                def parts(raw):
                    if kind < 2:
                        v = raw.rearrange("p (k n) -> p k n", k=4)
                        for n, w in enumerate((A["ffn_w_gate"], A["ffn_w_up"])):
                            yield (v[:, :, n * CW:(n + 1) * CW],
                                   w[l, half, kind * 512:kind * 512 + 512, bass.ds(c * CW, CW)]
                                   .rearrange("(k p) n -> p k n", p=P))
                    else:
                        for q in range(2):
                            yield (raw[:, q * D:(q + 1) * D],
                                   A["ffn_w_down"][l, half, bass.ds(c * CW + q * P, P), :])
                return parts

            sp.dma_start(cond[:, 0, :], A["c"][0].rearrange("(p k) -> p k", k=KD)).then_inc(cond_in, 16)
            for a in range(FIRST):
                if a >= ADA_RING:
                    sp.wait_ge(acc_step, a - ADA_RING + 1)
                k, cols, _ = first_piece(a)
                sp.dma_start(ada_raw[:, a % ADA_RING, :], ada[0, :, k, cols]).then_inc(first_full[a % ADA_RING], 16)
            for s, (kind, l, half) in enumerate(subs):
                if kind == "ffn":
                    def body(c0, i, loop):
                        for q in range(3):
                            load(base[s] + 3 * c0 + q, i, ffn_slot(l, half, q, c0 + 2 * i))
                    ffn_walk(sp, s, body)
                if kind == "mla":
                    with nc.allow_non_contiguous_dma(reason="few words"):
                        sp.wait_ge(diff_ready, 2)
                        sp.dma_start(pos_col[:, :], A["positions"][0].rearrange("(t p) -> p t", p=P)).then_inc(mla_in, 16)
                        for v, w in enumerate((A["mla_q_norm"], A["mla_kv_norm"])):
                            sp.dma_start(norm_col[:, 2 * v:2 * v + 2], w[0].rearrange("(k p) -> p k", p=P))\
                                .then_inc(mla_in, 16)
                    for n in range(2):
                        load(base[s] + n, 0, block(A["mla_w_down"][0], (n * 512, n * 512 + 512), 0, 512))
                    load(base[s] + 2, 0, block(A["mla_w_down"][0], (0, D), 512, 32))
                    for g in range(4):
                        load(base[s] + 3 + 2 * g, 0, block(A["mla_w_uq"][0], (0, 256), g * 384, 384))
                        load(base[s] + 4 + 2 * g, 0, block(A["mla_w_ukv"][0], (0, 256), g * 512, 512))
                    for n in range(4):
                        load(base[s] + MOUT + n, 0, block(A["mla_w_out"][0], (n * 256, n * 256 + 256), 0, D))
                if kind == "hyb":
                    win = A["hyb_w_in"][0]

                    def mixer_inputs():
                        sp.wait_ge(x_ready, 2 * s)
                        sp.dma_start(lb_logits, A["hgrn_lb_logits"].rearrange("(o a) n -> o a n", o=1)
                                     .broadcast_to([P, 3, 512])).then_inc(mix_in, 16)
                        sp.dma_start(pos_row, A["positions"].broadcast_to([P, SEQ])).then_inc(mix_in, 16)
                        with nc.allow_non_contiguous_dma(reason="256 words"):
                            sp.dma_start(pos_col[:, :], A["positions"][0].rearrange("(t p) -> p t", p=P))\
                                .then_inc(mix_in, 16)
                        sp.dma_start(sink_cols[:, :], A["attn_sink"].broadcast_to([P, 8])).then_inc(mix_in, 16)
                        sp.dma_start(norm_row, A["hgrn_norm_w"].rearrange("o h n -> o (h n)").broadcast_to([P, 512]))\
                            .then_inc(mix_in, 16)
                    for g, (c0, width) in enumerate(HG):
                        for n in range(width * KD // SLOT):
                            rows = (n * 512, n * 512 + 512) if width == 512 else (0, D)
                            load(base[s] + HG_SLOT[g] + n, 0, block(win, rows, c0, width))
                        if g == 2:
                            mixer_inputs()
                    for n in range(4):
                        load(base[s] + HOUT + n, 0, block(A["hyb_w_out"][0], (n * 256, n * 256 + 256), 0, D))
            for t in range(NT):
                sp.wait_ge(x_ready, 2 * last_sub + t + 1)
                sp.dma_start(out[0, t * P:(t + 1) * P, :], x[:, t, :]).then_inc(out_done, 16)
            sp.wait_ge(out_done, 32)

        @block.gpsimd
        def _(pool):
            step = Count(pool, pool_step)
            def ada_piece(s, n0, i):
                l, sub = divmod(s, N_SUB)
                a = ada_base(s) + n0
                if a >= ADA_RING:
                    pool.wait_ge(acc_step, a - ADA_RING + 1 + 12 * i)
                k, v = divmod(n0, 3)
                pool.dma_start(ada_raw[:, a % ADA_RING, :],
                               ada[l, :, k + 4 * i, sub * 3 * D + v * D:sub * 3 * D + (v + 1) * D])\
                    .then_inc(ada_full[a % ADA_RING], 16)

            def acc_start(s):
                if s == 1:
                    pool.wait_ge(ada_cols, 1)
                else:
                    pool.wait_ge(ada_gate, gate_base(s) if s > 2 else 2)
                nc.gpsimd.memset(acc, 0.0).then_inc(acc_init, 1)
                pool.wait_ge(acc_init, s + 1)
                l, sub = divmod(s, N_SUB)
                pool.dma_start(acc[0:1, :], A["ada_b"][l:l + 1, sub * 3 * D:(sub + 1) * 3 * D])\
                    .then_inc(acc_bias, 16)

            step(nc.gpsimd.memset(ident[:, :], 0.0))
            step.wait()
            nc.gpsimd.affine_select(out=ident[:, :], in_=ident[:, :], compare_op=ALU.not_equal, fill=1.0,
                                    base=0, pattern=[[-1, P]], channel_multiplier=1).then_inc(ident_ready, 1)
            nc.gpsimd.memset(ones[:, :], 1.0).then_inc(ident_ready, 1)
            nc.gpsimd.memset(neg_half[:, :], -0.5).then_inc(ident_ready, 1)
            pool.wait_ge(ident_ready, 3)
            for v, w in enumerate((A["ln_g"], A["ln_b"])):
                pool.dma_start(ln_nat[48 * v:48 * v + 48, :],
                               w.rearrange("l s (j p) -> (l s j) p", p=P)).then_inc(consts_in, 16)
            pool.dma_start(ln_nat[96:112, :], A["ada_b"][0, 0:2 * D].rearrange("(j p) -> j p", p=P))\
                .then_inc(consts_in, 16)
            pool.dma_start(x[:, 1, :], A["x"][0, P:2 * P, :]).then_inc(x_in[1], 16)

            def ln_tail(s):
                l, sub = divmod(s, N_SUB)
                if subs[s][0] == "hyb":
                    pool.wait_ge(ho_done, 8)
                elif subs[s][0] == "mla":
                    pool.wait_ge(o_ready, O0 + 4)
                for v, w in enumerate((A["ln_g"], A["ln_b"])):
                    pool.dma_start(ln_rows[:, v, :], w[l, sub:sub + 1, :].broadcast_to([P, D]))\
                        .then_inc(ln_rows_in, 16)
                for t in range(NT):
                    u = 2 * s + t
                    pool.wait_ge(var_ready, u + 1)
                    nc.gpsimd.tensor_tensor(rstd[:, :], var_eps[:, :], neg_half[:, :], ALU.pow).then_inc(rstd_ready, 1)
                    pool.wait_ge(n_ready, u + 1)
                    if s < last_sub:
                        pool.wait_ge(n_tr, 2 * (u + 3))
                    elif t == NT - 1:
                        break
                    pool.wait_ge(ln_rows_in, 32 * (s + 1))
                    step(nc.gpsimd.tensor_tensor(x[:, t, :], x[:, t, :], ln_rows[:, 0, :], ALU.mult))
                    step.wait()
                    nc.gpsimd.tensor_tensor(x[:, t, :], x[:, t, :], ln_rows[:, 1, :], ALU.add).then_inc(x_ready, 1)
                if s < last_sub:
                    pool.wait_ge(x_ready, 2 * (s + 1))

            for s, (kind, _, _) in enumerate(subs):
                if kind == "ffn":
                    for loop, nxt in enumerate(ada_plan[s]):
                        acc_start(nxt)
                        if loop == 0:
                            pool.wait_ge(h_ready, 4 * s + 4)
                        with pool.Fori(0, 2) as i:
                            for n in range(12):
                                ada_piece(nxt, n, i)
                        if s == 0 and loop == 0:
                            for k in range(KD):
                                a = GATE0 + k
                                pool.wait_ge(acc_step, a - ADA_RING + 1)
                                pool.dma_start(ada_raw[:, a % ADA_RING, :], ada[0, :, k, 2 * D:3 * D])\
                                    .then_inc(ada_full[a % ADA_RING], 16)
                if kind == "hyb":
                    pool.wait_ge(y_ready, 2 * s)
                    F, B = tri[:, 0, 0, :], tri[:, 1, 0, :]
                    step(nc.gpsimd.memset(tri[:, :, 0, :], 1.0))
                    step(nc.gpsimd.memset(half_sel[:, :], 0.0))
                    step.wait()
                    step(nc.gpsimd.affine_select(out=F, in_=F, compare_op=ALU.is_ge, fill=0.0, base=0,
                                                 pattern=[[1, P]], channel_multiplier=-1))
                    step(nc.gpsimd.affine_select(out=B, in_=B, compare_op=ALU.is_ge, fill=0.0, base=0,
                                                 pattern=[[-1, P]], channel_multiplier=1))
                    step.wait()
                    step(nc.gpsimd.memset(F[0:64, 64:128], 0.0))
                    step(nc.gpsimd.memset(B[64:128, 0:64], 0.0))
                    step(nc.gpsimd.memset(half_sel[0:64, 0:1], 1.0))
                    step(nc.gpsimd.memset(half_sel[64:128, 1:2], 1.0))
                    step.wait()
                    step(nc.gpsimd.tensor_copy(tri[:, 0, 1, :], F))
                    step(nc.gpsimd.tensor_copy(tri[:, 1, 1, :], B))
                    step(nc.gpsimd.tensor_tensor(tri[:, 0, 2, :], B, ident[:, :], ALU.subtract))
                    step(nc.gpsimd.tensor_tensor(tri[:, 1, 2, :], F, ident[:, :], ALU.subtract))
                    step.wait()
                    for j in range(2):
                        for d in range(2):
                            blk = tri[64 * j + 32 * d:64 * j + 32 * d + 32, d, 1, 64 * j:64 * j + 64]
                            step(nc.gpsimd.tensor_scalar(blk, blk, -1.0, None, ALU.add))
                    step.wait()
                    pool.sem_inc(tri_ready, 1)
                    pool.wait_ge(mix_in, 80)
                    for t in range(NT):
                        nc.gpsimd.tensor_tensor(dist[:, t, :].bitcast(I32), pos_row,
                                                pos_col[:, t:t + 1].broadcast_to([P, SEQ]), ALU.subtract)\
                            .then_inc(diff_ready, 1)
                    pool.wait_ge(dist_abs, 1)
                    for t in range(NT):
                        nc.gpsimd.affine_select(out=dist[:, t, :], in_=dist[:, t, :], compare_op=ALU.is_ge,
                                                fill=1e30, base=P if t == 0 else 0,
                                                pattern=[[-1 if t == 0 else 1, SEQ]],
                                                channel_multiplier=1 if t == 0 else -1).then_inc(dist_ready, 1)
                    pool.wait_ge(lb_max, 1)
                    for v in range(3):
                        op = nc.gpsimd.tensor_tensor(lb_logits[:, v, :], lb_logits[:, v, :], lb_tmp, ALU.subtract)
                    op.then_inc(lb_pre, 1)
                    pool.wait_ge(lb_exp, 1)
                    step(nc.gpsimd.tensor_tensor(lb_tmp, lb_logits[:, 0, :], lb_logits[:, 1, :], ALU.add))
                    step.wait()
                    nc.gpsimd.tensor_tensor(lb_tmp, lb_tmp, lb_logits[:, 2, :], ALU.add).then_inc(lb_sum, 1)
                    pool.wait_ge(lb_rec, 1)
                    step(nc.gpsimd.tensor_tensor(lb_rows[:, 0, :], lb_logits[:, 0, :], lb_tmp, ALU.mult))
                    step.wait()
                    nc.gpsimd.tensor_scalar(lb_rows[:, 1, :], lb_rows[:, 0, :], -1.0, 1.0, ALU.mult, ALU.add)\
                        .then_inc(lb_rows_ready, 1)
                    pool.wait_ge(lb_rows_ready, 1)
                    for stage, m in hybrid_plan():
                        if stage == "sig":
                            pool.wait_ge(sig_ready, 1)
                            for d, t in HSTEP:
                                step(nc.gpsimd.tensor_tensor(hf[:, d, t, :], hf[:, d, t, :], lb_rows[:, 1, :], ALU.mult))
                                step.wait()
                                nc.gpsimd.tensor_tensor(hf[:, d, t, :], hf[:, d, t, :], lb_rows[:, 0, :], ALU.add)\
                                    .then_inc(f_ready, 1)
                        elif stage == "proj" and m[0] == 6:
                            pool.wait_ge(proj_read, 2 * m[0] + m[1] + 1)
                            nc.gpsimd.tensor_tensor(hg_gate[:, m[1], :], hg_gate[:, m[1], :], norm_row, ALU.mult)\
                                .then_inc(gate_mul, 1)
                        elif stage == "cum":
                            d, t = HSTEP[m]
                            pool.wait_ge(logf_ready, m + 1)
                            nc.gpsimd.tensor_scalar(hf[:, d, t, :], hf[:, d, t, :], -1.0, 1.0, ALU.mult, ALU.add)\
                                .then_inc(k_ready, 1)
                        elif stage in ("prod", "turn"):
                            d, t = HSTEP[m]
                            if stage == "prod":
                                n, e = 2, 1
                                pool.wait_ge(k_ready, m + 1)
                            else:
                                n, e = 4, 3
                                if m == 0:
                                    pool.wait_ge(o_att, 8)
                                if m > 0:
                                    pool.wait_ge(ho_done, 2 * m)
                                nc.gpsimd.memset(hA[:, :, :], 0.0).then_inc(hA_zero, 1)
                            pool.wait_ge(hexp_ready, 5 * m + n)
                            nc.gpsimd.tensor_tensor(hexp[:, e, :], hexp[:, e, :], hf[:, d, t, :], ALU.mult)\
                                .then_inc(ke_ready, 1)
                        elif stage == "hnorm":
                            pool.wait_ge(ms_ready, m + 1)
                            nc.gpsimd.tensor_tensor(rms[:, 4 * m:4 * m + 4], ssq[:, 4 * m:4 * m + 4],
                                                    neg_half[:, 0:1].broadcast_to([P, 4]), ALU.pow).then_inc(rms_ready, 1)
                if kind == "mla":
                    pool.wait_ge(y_ready, 2 * s)
                    for n in range(16):
                        op = nc.gpsimd.memset(freq[:, n:n + 1], float(np.float32(10000.0) ** np.float32(-n / 16)))
                    op.then_inc(freq_ready, 1)

                    def rotate(x, t, done, outs):
                        h = x.shape[1]
                        cos, sin = (rot[:, v, t:t + 1, :].broadcast_to([P, h, 16]) for v in range(2))
                        a, b = x[:, :, 0:16], x[:, :, 16:32]
                        for n, (u, v) in enumerate(((a, cos), (b, sin), (a, sin), (b, cos))):
                            step(nc.gpsimd.tensor_tensor(rp[:, n, 0:h, :], u, v, ALU.mult))
                        step.wait()
                        for out in outs:
                            nc.gpsimd.tensor_tensor(out[:, :, 0:16], rp[:, 0, 0:h, :], rp[:, 1, 0:h, :], ALU.subtract)
                            op = nc.gpsimd.tensor_tensor(out[:, :, 16:32], rp[:, 2, 0:h, :], rp[:, 3, 0:h, :], ALU.add)
                        op.then_inc(done, 1)

                    for stage, m in mla_plan():
                        if stage == "cn":
                            t = m
                            pool.wait_ge(ms_ready, R0 + t + 1)
                            nc.gpsimd.tensor_tensor(rms[:, 2 * t:2 * t + 2], ssq[:, 2 * t:2 * t + 2],
                                                    neg_half[:, 0:1].broadcast_to([P, 2]), ALU.pow).then_inc(rms_ready, 1)
                        elif stage == "kr":
                            t = m[1]
                            if t == 0:
                                pool.wait_ge(rot_ready, 1)
                            pool.wait_ge(proj_read, P0 + mla_piece(stage, m) + 1)
                            if t == 1:
                                pool.wait_ge(kr_done, 1)
                            rotate(kr_nat[:, t:t + 1, :], t, kr_done, [k_nat[:, t, h:h + 1, 64:96] for h in range(4)])
                        elif stage == "uq":
                            g, t = m
                            pool.wait_ge(proj_read, P0 + mla_piece(stage, m) + 1)
                            if g == 0 and t == 0:
                                pool.wait_ge(kr_done, 2)
                            else:
                                pool.wait_ge(q_rot, 2 * g + t)
                            x_rope = q_nat[:, t, :, 64:96]
                            rotate(x_rope, t, q_rot, [x_rope])
                ln_tail(s)

        @block.scalar
        def _(act):
            def split_hi(j0, i):
                if isinstance(i, int) and j0 >= ALL_SLOTS:
                    return
                act.wait_ge(raw_full[j0 % RAW], 32 * (j0 // RAW + 1 + RING // RAW * i))
                if j0 >= RING:
                    act.wait_ge(slot_used, j0 - RING + 1 + RING * i)
                n = slot_size(j0)
                nc.scalar.activation(w_hi[:, j0 % RING, 0:n], w_raw[:, j0 % RAW, 0:n], ACT.Copy).then_inc(hi_ready, 1)

            def enter(s, t, between=None):
                u = 2 * s + t
                act.wait_ge(n_tr, 2 * u + 1)
                if t == 0:
                    act.wait_ge(mods_ready, s + 1)
                if u > 0:
                    act.wait_ge(h_ready, 2 * u)
                for half in range(2):
                    for k in (4 * half, 4 * half + 1):
                        c = turned(k)
                        mm = nc.scalar.activation(scratch[:, k * P:(k + 1) * P], entry_banks(s, t)[0][:, c], ACT.Identity,
                                                  bias=mod_B[:, s, k:k + 1], scale=mod_G[:, s, k:k + 1])
                    mm.then_inc(hf_act, 1)
                    act.wait_ge(hf_act, 2 * u + half + 1)
                    act.wait_ge(hf_dve, 2 * u + half + 1)
                    nc.scalar.activation(hT_hi[:, 4 * half:4 * half + 4, t * P:(t + 1) * P],
                                         scratch[:, half * 512:half * 512 + 512].rearrange("p (k n) -> p k n", k=4),
                                         ACT.Copy).then_inc(h_hi_ready, 1)
                    if half == 0 and between is not None:
                        between()

            def attention_exp(m):
                act.wait_ge(s_max, m + 1)
                if m >= 4:
                    act.wait_ge(o_att, m - 3)
                for a in range(2):
                    op = nc.scalar.activation(win_s[:, m % 2, a, :], win_s[:, m % 2, a, :], ACT.Exp,
                                              bias=neg_max[:, m % 2, a:a + 1], accum_out=den[:, m % 4, a:a + 1])
                op.then_inc(s_exp, 1)

            def gate_half(s, half, bank):
                w = 0.5 if subs[s][0] == "ffn" else 1.0
                act.wait_ge(ada_gate, gate_base(s) + 2 - half)
                nc.scalar.activation(gate_row[:, s % 3, half * 512:half * 512 + 512], bank[:, :], ACT.Copy,
                                     bias=w, scale=w).then_inc(gate_ready, 1)

            act.dma_start(x[:, 0, :], A["x"][0, 0:P, :]).then_inc(x_in[0], 16)
            act.wait_ge(cond_in, 16)
            nc.scalar.activation(cond[:, 1, :], cond[:, 0, :], ACT.Silu).then_inc(cond_ready, 1)
            act.wait_ge(acc_init, 1)
            act.dma_start(acc_gate0[0:1, :], A["ada_b"][0:1, 2 * D:3 * D]).then_inc(gate_bias, 16)
            split_hi(0, 0)
            for s, (kind, _, _) in enumerate(subs):
                if kind == "ffn":
                    def silu(t, u):
                        act.wait_ge(gu_done, u + 1)
                        nc.scalar.activation(sg[:, t, :], G[t][:, 0:CW], ACT.Silu).then_inc(silu_done, 1)

                    def take_hi(t, u):
                        act.wait_ge(hid_tr, u + 1)
                        nc.scalar.activation(fT_hi[:, t, :], T[t][:, 0:CW], ACT.Copy).then_inc(fT_hi_ready, 1)

                    enter(s, 0)
                    if s == 0:
                        split_hi(1, 0)
                        split_hi(2, 0)
                    silu(0, ffn_units[s])
                    enter(s, 1, lambda: take_hi(0, ffn_units[s]))

                    def body(c0, i, loop):
                        u = ffn_units[s] + 2 * c0 + 4 * i
                        nxt = base[s] + 3 * (c0 + 1)
                        fin = None if loop is not None else fin_of(s, c0)
                        for t in range(NT):
                            ahead = t == 0 and c0 == 0
                            if not ahead:
                                silu(t, u + t)
                            if t == 1 and fin is not None:
                                gate_half(fin, 0, T[0])
                            if t == 0 or c0 < NCH - 1:
                                split_hi(nxt + 2 * t, i)
                            if not ahead:
                                take_hi(t, u + t)
                            if t == 0:
                                if fin is not None:
                                    gate_half(fin, 1, G[0])
                                split_hi(nxt + 1, i)
                                if c0 == NCH - 1:
                                    split_hi(nxt + 2, i)
                            elif fin == 1:
                                gate_half(0, 1, G[1])
                                gate_half(0, 0, T[1])
                    ffn_walk(act, s, body)
                if kind == "mla":
                    for stage, m in mla_plan():
                        if stage == "enter":
                            enter(s, m)
                            if m == 1:
                                act.wait_ge(angle_ready, 1)
                                nc.scalar.activation(rot[:, :, :, :], angle[:, :, :, :], ACT.Sin).then_inc(rot_ready, 1)
                        elif stage == "cn":
                            t = m
                            act.wait_ge(proj_done, P0 + t + 1)
                            nc.scalar.activation(c_tmp[:, t, :], banks[t][:, :], ACT.Square).then_inc(sq_ready, 1)
                        elif stage == "cT":
                            act.wait_ge(c_tr, m + 1)
                            for k in range(4):
                                op = nc.scalar.activation(c_tmp[:, m, k * P:(k + 1) * P], banks[6 + m][:, k * P:(k + 1) * P],
                                                          ACT.Copy, scale=norm_col[:, k:k + 1])
                            op.then_inc(c_mul, 1)
                            act.wait_ge(c_mul, m + 1)
                            nc.scalar.activation(hT_hi[:, 0:4, m * P:(m + 1) * P],
                                                 c_tmp[:, m, :].rearrange("p (k n) -> p k n", k=4), ACT.Copy)\
                                .then_inc(c_hi, 1)
                        elif stage == "uq":
                            g, t = m
                            act.wait_ge(proj_done, P0 + mla_piece(stage, m) + 1)
                            if g > 0:
                                act.wait_ge(qk4_tr, 2 * (g - 1) + t + 1)
                            nc.scalar.activation(q_nat[:, t, :, :], mla_bank(stage, t)[:, 0:384].rearrange("p (h n) -> p h n", h=4),
                                                 ACT.Copy, scale=MLA_SCALE).then_inc(proj_read, 1)
                        elif stage == "ukv":
                            g, t = m
                            act.wait_ge(proj_done, P0 + mla_piece(stage, m) + 1)
                            if g >= 2:
                                act.wait_ge(pv_done, A0 + 4 * (g - 1))
                            kv = mla_bank(stage, t)[:, :].rearrange("p (h n) -> p h n", h=4)
                            nc.scalar.activation(k_nat[:, t, :, 0:64], kv[:, :, 0:64], ACT.Copy)
                            nc.scalar.activation(v_nat[:, g % 2, t, :].rearrange("p (h n) -> p h n", h=4), kv[:, :, 64:128],
                                                 ACT.Copy).then_inc(proj_read, 1)
                        elif stage == "S":
                            b = m % 2
                            act.wait_ge(s_max, A0 + m + 1)
                            if m >= 2:
                                act.wait_ge(p_tr, A0 + m - 1)
                            if m >= 4:
                                act.wait_ge(o_att, A0 + m - 3)
                            if m == 0:
                                act.wait_ge(cT_ready, 2)
                            for a in range(2):
                                op = nc.scalar.activation(mP[:, b, a, :], banks[2 + b][:, a * SEQ:(a + 1) * SEQ], ACT.Exp,
                                                          bias=neg_max[:, b, a:a + 1], accum_out=den[:, m % 4, a:a + 1])
                            op.then_inc(s_exp, 1)
                        elif stage == "V":
                            g, t, p = m // 4, m % 4 // 2, m % 2
                            act.wait_ge(pv_done, A0 + m + 1)
                            act.wait_ge(rden_ready, m + 1)
                            for a in range(2):
                                h = 4 * g + 2 * p + a
                                op = nc.scalar.activation(m_o[:, t, h * 64:h * 64 + 64], banks[5][:, a * 64:a * 64 + 64],
                                                          ACT.Copy, scale=rden[:, m % 4, a:a + 1])
                            op.then_inc(o_att, 1)
                        elif stage == "owin":
                            t, half = m
                            if m == (0, 0):
                                act.wait_ge(proj_done, P0 + 20)
                            act.wait_ge(o_tr, O0 + 2 * half + t + 1)
                            nc.scalar.activation(hT_hi[:, 4 * half:4 * half + 4, t * P:(t + 1) * P],
                                                 banks[6 + t][:, :].rearrange("p (k n) -> p k n", k=4), ACT.Copy)\
                                .then_inc(o_hi, 1)
                        for n in mla_split(stage, m):
                            split_hi(base[s] + n, 0)
                if kind == "hyb":
                    for stage, m in hybrid_plan():
                        if stage == "enter":
                            enter(s, m)
                        elif stage == "dist":
                            act.wait_ge(diff_ready, 2)
                            nc.scalar.activation(dist[:, :, :], dist[:, :, :].bitcast(I32), ACT.Abs).then_inc(dist_abs, 1)
                        elif stage == "lb" and m == 0:
                            act.wait_ge(lb_pre, 1)
                            nc.scalar.activation(lb_logits, lb_logits, ACT.Exp).then_inc(lb_exp, 1)
                        elif stage == "proj":
                            g, t = m
                            act.wait_ge(proj_done, 2 * g + t + 1)
                            b = Y[0][t]
                            if g == 0:
                                kk = b[:, 0:128].rearrange("p (g n) -> p g n", g=2)
                                for c in range(2):
                                    nc.scalar.activation(k_dup[:, t, :, c * 64:c * 64 + 64], kk, ACT.Copy)
                                op = nc.scalar.activation(va[:, t, :], b[:, 128:256], ACT.Copy)
                            elif g == 1:
                                op = nc.scalar.activation(qa[:, t, :], b[:, :], ACT.Copy, scale=0.125)
                            elif g in (2, 3):
                                if (g, t) == (3, 1):
                                    act.wait_ge(lb_rows_ready, 1)
                                op = nc.scalar.activation(hf[:, g - 2, t, :], b[:, :], ACT.Copy)
                            elif g == 4:
                                op = nc.scalar.activation(hq[:, t, :], b[:, :], ACT.Copy)
                            elif g == 5:
                                op = nc.scalar.activation(hv[:, t, :], b[:, :], ACT.Copy)
                            else:
                                if t == 0:
                                    act.wait_ge(f_ready, 4)
                                op = nc.scalar.activation(hg_gate[:, t, :], b[:, :], ACT.Silu)
                            op.then_inc(proj_read, 1)
                            if g == 6 and t == 0:
                                act.wait_ge(proj_read, 10)
                                nc.scalar.activation(hq[:, :, :], hq[:, :, :], ACT.Silu).then_inc(hq_ready, 1)
                        elif stage == "split":
                            split_hi(base[s] + 2 * m[0] + m[1] + 2, 0)
                        elif stage == "sig":
                            act.wait_ge(proj_read, 8)
                            nc.scalar.activation(hf[:, :, :, :], hf[:, :, :, :], ACT.Sigmoid).then_inc(sig_ready, 1)
                        elif stage == "qk":
                            for n in range(2):
                                act.wait_ge(qk_tr, n + 1)
                                nc.scalar.activation(qT[:, 2 * n:2 * n + 2, :], G[n][:, :], ACT.Copy).then_inc(qk_act, 1)
                        elif stage == "S":
                            attention_exp(m)
                        elif stage == "P":
                            act.wait_ge(p_tr, m + 1)
                            if m >= 2:
                                act.wait_ge(pv_done, m - 1)
                            nc.scalar.activation(win_pT[:, m % 2, :], banks[6][:, :], ACT.Copy).then_inc(pT_ready, 1)
                        elif stage == "owin":
                            act.wait_ge(o_tr, m + 1)
                            nc.scalar.activation(hT_hi[:, 0:4, m * P:(m + 1) * P],
                                                 banks[m][:, :].rearrange("p (k n) -> p k n", k=4), ACT.Copy)\
                                .then_inc(o_hi, 1)
                        elif stage == "log":
                            act.wait_ge(f_ready, 4)
                            act.wait_ge(o_att, 8)
                            act.wait_ge(gate_mul, 2)
                            act.wait_ge(o_tr, 2)
                            for n, (d, t) in enumerate(HSTEP):
                                nc.scalar.activation(logf[n], hf[:, d, t, :], ACT.Ln).then_inc(logf_ready, 1)
                        elif stage == "cum" and m > 0:
                            split_hi(base[s] + 15 + m, 0)
                        elif stage in ("prod", "turn"):
                            for n, (e, src, scale) in enumerate(((0, 4, 1.0), (1, 4, -1.0), (2, 5, 1.0), (3, 6, 1.0))):
                                if (n == 3) != (stage == "turn"):
                                    continue
                                act.wait_ge(cum_done, 4 * m + (1, 1, 2, 3)[n])
                                if n == 0 and m > 0:
                                    act.wait_ge(he_tr, 3 * m)
                                if n == 3 and m > 0:
                                    act.wait_ge(dS_done, dS_before(m))
                                nc.scalar.activation(hexp[:, e, :], banks[src][:, :], ACT.Exp, scale=scale)\
                                    .then_inc(hexp_ready, 1)
                            if stage == "prod":
                                continue
                            act.wait_ge(cum_done, 4 * m + 4)
                            if m > 0:
                                act.wait_ge(S_ready, dS_before(m))
                            nc.scalar.activation(decay[:, :], banks[7][:, 0:8], ACT.Exp).then_inc(hexp_ready, 1)
                        elif stage == "hnorm":
                            if m == 0:
                                act.wait_ge(ho_done, 8)
                            nc.scalar.activation(hexp[:, m, :], banks[2 + m][:, :], ACT.Square).then_inc(sq_ready, 1)
                            act.wait_ge(o_tr, 2 + m + 1)
                            nc.scalar.activation(hT_hi[:, 4:8, m * P:(m + 1) * P],
                                                 banks[4 + m][:, :].rearrange("p (k n) -> p k n", k=4), ACT.Copy)\
                                .then_inc(o_hi, 1)
                        elif stage == "out" and m == (0, 1):
                            split_hi(base[s] + 19, 0)

        @block.vector
        def _(dve):
            step = Count(dve, dve_step)

            def split_lo(j0, i):
                if isinstance(i, int) and j0 >= ALL_SLOTS:
                    return
                dve.wait_ge(hi_ready, j0 + 1 + RING * i)
                n = slot_size(j0)
                nc.vector.tensor_tensor(w_lo[:, j0 % RING, 0:n], w_raw[:, j0 % RAW, 0:n],
                                        w_hi[:, j0 % RING, 0:n].bitcast(F32), ALU.subtract)\
                    .then_inc(lo_ready[j0 % RING], 1)

            def ada_piece(s, n0, i):
                a = ada_base(s) + n0
                k, v = divmod(n0, 3)
                dve.wait_ge(ada_full[a % ADA_RING], 16 * ((a - FIRST) // ADA_RING + 1 + 3 * i))
                if n0 == 0:
                    dve.wait_ge(acc_bias, 16 * s)
                if a > 2:
                    dve.wait_ge(acc_step, a - 2 + 12 * i)
                nc.vector.scalar_tensor_tensor(out=acc[:, v * D:(v + 1) * D], in0=ada_raw[:, a % ADA_RING, :],
                                               scalar=cond[:, 1, bass.ds(k + 4 * i, 1)], in1=acc[:, v * D:(v + 1) * D],
                                               op0=ALU.mult, op1=ALU.add).then_inc(acc_step, 1)

            def enter(s, t, between=None):
                u = 2 * s + t
                dve.wait_ge(n_tr, 2 * u + 2)
                if u > 0:
                    dve.wait_ge(h_ready, 2 * u)
                if t == 0:
                    dve.wait_ge(mods_ready, s + 1)
                for half in range(2):
                    for k in (4 * half + 2, 4 * half + 3):
                        op = nc.vector.tensor_scalar(scratch[:, k * P:(k + 1) * P], entry_banks(s, t)[1][:, turned(k)],
                                                     mod_G[:, s, k:k + 1], mod_B[:, s, k:k + 1], ALU.mult, ALU.add)
                    op.then_inc(hf_dve, 1)
                if between is not None:
                    between()
                for half in range(2):
                    dve.wait_ge(h_hi_ready, 2 * u + half + 1)
                    ks = slice(4 * half, 4 * half + 4)
                    nc.vector.tensor_tensor(hT_lo[:, ks, t * P:(t + 1) * P],
                                            scratch[:, half * 512:half * 512 + 512].rearrange("p (k n) -> p k n", k=4),
                                            hT_hi[:, ks, t * P:(t + 1) * P].bitcast(F32), ALU.subtract)\
                        .then_inc(h_ready, 1)

            def mods(s, bank):
                dve.wait_ge(ada_cols, s + 1)
                if s == 0:
                    nc.vector.scalar_tensor_tensor(out=mod_G[:, 0, :], in0=bank[:, 8:16], scalar=1.0,
                                                   in1=ln_col[:, 104:112], op0=ALU.add, op1=ALU.add)
                    nc.vector.tensor_tensor(mod_B[:, 0, :], bank[:, 0:8], ln_col[:, 96:104], ALU.add)\
                        .then_inc(mods_ready, 1)
                    return
                step(nc.vector.tensor_scalar(mod_1s[:, :], bank[:, 8:16], 1.0, None, ALU.add))
                step.wait()
                g, b = ln_col[:, (s - 1) * 8:s * 8], ln_col[:, 48 + (s - 1) * 8:48 + s * 8]
                nc.vector.tensor_tensor(mod_G[:, s, :], mod_1s[:, :], g, ALU.mult)
                step(nc.vector.tensor_tensor(mod_B[:, s, :], mod_1s[:, :], b, ALU.mult))
                step.wait()
                nc.vector.tensor_tensor(mod_B[:, s, :], mod_B[:, s, :], bank[:, 0:8], ALU.add).then_inc(mods_ready, 1)

            def residual(s, t):
                u = 2 * s + t
                dve.wait_ge(y_ready, u + 1)
                if t == 0:
                    dve.wait_ge(gate_ready, max(gate_base(s) + 2, 4))
                if s > 0:
                    dve.wait_ge(x_ready, 2 * (s - 1) + t + 1)
                dve.wait_ge(h_ready, 2 * (2 * s + 2 + (t == 1 and s < last_sub)))
                for half in range(2):
                    c = slice(half * 512, half * 512 + 512)
                    step(nc.vector.tensor_tensor(scratch[:, c], Y[t][half][:, :], gate_row[:, s % 3, c], ALU.mult))
                for half in range(2):
                    c = slice(half * 512, half * 512 + 512)
                    dve.wait_ge(dve_step, step.n - 1)
                    step(nc.vector.scalar_tensor_tensor(out=x[:, t, c], in0=x[:, t, c], scalar=ALPHA,
                                                        in1=scratch[:, c], op0=ALU.mult, op1=ALU.add))

            def norm(s, t):
                u = 2 * s + t
                for half in range(2):
                    c = slice(half * 512, half * 512 + 512)
                    dve.wait_ge(dve_step, step.n - 1)
                    step(nc.vector.bn_stats(stats[:, half, :], x[:, t, c]))
                step.wait()
                step(nc.vector.bn_aggr(mean_var[:, :], stats[:, :, :]))
                step.wait()
                nc.vector.tensor_scalar(var_eps[:, :], mean_var[:, 1:2], LN_EPS, None, ALU.add).then_inc(var_ready, 1)
                dve.wait_ge(rstd_ready, u + 1)
                nc.vector.tensor_scalar(x[:, t, :], x[:, t, :], mean_var[:, 0:1], rstd[:, 0:1],
                                        ALU.subtract, ALU.mult).then_inc(n_ready, 1)

            def hybrid(s):
                for stage, m in hybrid_plan():
                    if stage == "enter":
                        if m == 1:
                            enter(s, 1)
                    elif stage == "dist":
                        dve.wait_ge(mix_in, 80)
                        step(nc.vector.tensor_tensor(lb_tmp, lb_logits[:, 0, :], lb_logits[:, 1, :], ALU.max))
                        step.wait()
                        nc.vector.tensor_tensor(lb_tmp, lb_tmp, lb_logits[:, 2, :], ALU.max).then_inc(lb_max, 1)
                    elif stage == "lb":
                        if m == 1:
                            dve.wait_ge(lb_sum, 1)
                            nc.vector.reciprocal(lb_tmp, lb_tmp).then_inc(lb_rec, 1)
                    elif stage == "split":
                        split_lo(base[s] + 2 * m[0] + m[1] + 2, 0)
                    elif stage == "qk":
                        dve.wait_ge(qk_tr, 3)
                        nc.vector.tensor_copy(kT[:, :, :], banks[6][:, :].rearrange("p (g n) -> p g n", g=2))\
                            .then_inc(qk_dve, 1)
                        dve.wait_ge(dist_ready, 2)
                    elif stage == "S":
                        t, p = divmod(m, 4)
                        b = m % 2
                        dve.wait_ge(s_done, m + 1)
                        if m == 0:
                            dve.wait_ge(qk_act, 2)
                        if m >= 2:
                            dve.wait_ge(p_tr, m - 1)
                        for a in range(2):
                            h = 2 * p + a
                            nc.vector.scalar_tensor_tensor(out=win_s[:, b, a, 0:SEQ], in0=dist[:, t, :],
                                                           scalar=-2.0 ** -(h + 1),
                                                           in1=banks[2 + 2 * b + a][:, 0:SEQ],
                                                           op0=ALU.mult, op1=ALU.add)
                        step(nc.vector.tensor_copy(win_s[:, b, :, SEQ], sink_cols[:, 2 * p:2 * p + 2]))
                        step.wait()
                        nc.vector.tensor_reduce(neg_max[:, b, :], win_s[:, b, :, :], AX.X, ALU.max, negate=True)\
                            .then_inc(s_max, 1)
                    elif stage == "V":
                        t, p = divmod(m, 4)
                        b = m % 4
                        dve.wait_ge(s_exp, m + 1)
                        if m >= 4:
                            dve.wait_ge(o_att, m - 3)
                        step(nc.vector.reciprocal(rden[:, b, :], den[:, b, :]))
                        dve.wait_ge(pv_done, m + 1)
                        step.wait()
                        for a in range(2):
                            h = 2 * p + a
                            op = nc.vector.tensor_scalar(o_win[:, t, h * 64:h * 64 + 64],
                                                         banks[7][:, a * 64:a * 64 + 64], rden[:, b, a:a + 1],
                                                         None, ALU.mult)
                        op.then_inc(o_att, 1)
                    elif stage == "owin":
                        out_lo(m, 0, banks[m], m)
                    elif stage == "cum" and m > 0:
                        split_lo(base[s] + 15 + m, 0)
                    elif stage in ("prod", "turn"):
                        if stage == "prod":
                            if m == 0:
                                dve.wait_ge(hq_ready, 1)
                            for n, e in ((1, 0), (3, 2)):
                                dve.wait_ge(hexp_ready, 5 * m + n)
                                nc.vector.tensor_tensor(hexp[:, e, :], hexp[:, e, :], hq[:, HSTEP[m][1], :], ALU.mult)\
                                    .then_inc(qe_ready, 1)
                        for n, b in ((0, 4), (1, 5)) if stage == "prod" else ((2, 6),):
                            dve.wait_ge(he_tr, 3 * m + n + 1)
                            if n == 2 and m > 0:
                                dve.wait_ge(ho_done, 2 * m)
                            nc.vector.tensor_copy(hexpT[:, n, :], banks[b][:, :]).then_inc(heT_dve, 1)
                        if stage == "prod":
                            continue
                        dve.wait_ge(hA_done, m + 1)
                        dve.wait_ge(hA_zero, m + 1)
                        d = HSTEP[m][0]
                        for j in range(2):
                            rows = slice(64 * j, 64 * j + 64)
                            mask = tri[rows, d, 0, 64 * j:64 * j + 64].bitcast(I32)
                            for h in range(4):
                                op = nc.vector.copy_predicated(hA[rows, h, :], mask,
                                                               banks[0][rows, h * 64:h * 64 + 64])
                        op.then_inc(hA_ready, 1)
                    elif stage == "chain":
                        d, t = HSTEP[m]
                        for jj in range(2):
                            n = dS_index(m, jj)
                            if n is None:
                                continue
                            j = jj if d == 0 else 1 - jj
                            dve.wait_ge(dS_done, n + 1)
                            if jj == 0 and m < 2:
                                nc.vector.tensor_copy(hS[:, d, :], banks[1][:, :]).then_inc(S_ready, 1)
                                continue
                            dve.wait_ge(hexp_ready, 5 * (m + 1))
                            dve.wait_ge(S_ready, S_last(m, jj))
                            dve.wait_ge(ho_done, 2 * m + jj + 1)
                            for h in range(4):
                                c = slice(h * P, (h + 1) * P)
                                op = nc.vector.scalar_tensor_tensor(out=hS[:, d, c], in0=hS[:, d, c],
                                                                    scalar=decay[:, 2 * h + j:2 * h + j + 1],
                                                                    in1=banks[1][:, c], op0=ALU.mult, op1=ALU.add)
                            op.then_inc(S_ready, 1)
                    elif stage == "hnorm":
                        dve.wait_ge(sq_ready, m + 1)
                        step(nc.vector.tensor_reduce(ssq[:, 4 * m:4 * m + 4],
                                                     hexp[:, m, :].rearrange("p (h n) -> p h n", h=4), AX.X, ALU.add))
                        step.wait()
                        nc.vector.tensor_scalar(ssq[:, 4 * m:4 * m + 4], ssq[:, 4 * m:4 * m + 4], 1.0 / P, RMS_EPS,
                                                ALU.mult, ALU.add).then_inc(ms_ready, 1)
                        dve.wait_ge(rms_ready, m + 1)
                        dve.wait_ge(gate_mul, m + 1)
                        for h in range(4):
                            c = slice(h * P, (h + 1) * P)
                            op = nc.vector.scalar_tensor_tensor(out=hq[:, m, c], in0=banks[2 + m][:, c],
                                                                scalar=rms[:, 4 * m + h:4 * m + h + 1],
                                                                in1=hg_gate[:, m, c], op0=ALU.mult, op1=ALU.mult)
                        op.then_inc(ho_ready, 1)
                        out_lo(2 + m, 4, banks[4 + m], m)
                    elif stage == "out" and m == (0, 1):
                        split_lo(base[s] + 19, 0)

            def mla(s):
                for stage, m in mla_plan():
                    if stage == "enter":
                        if m == 1:
                            enter(s, 1)
                            dve.wait_ge(mla_in, 48)
                            dve.wait_ge(freq_ready, 1)
                            for t in range(NT):
                                step(nc.vector.tensor_copy(turns[:, 0, t, 0:1], pos_col[:, t:t + 1]))
                            step.wait()
                            for t in range(NT):
                                for v in range(2):
                                    op = nc.vector.tensor_scalar(angle[:, v, t, :], freq[:, :], turns[:, 0, t, 0:1], None, ALU.mult)
                            step(op)
                            step.wait()
                            for v in range(2):
                                op = nc.vector.tensor_scalar(turns[:, v, :, :], angle[:, v, :, :], 0.5 / math.pi, (0.25, 0.0)[v],
                                                             ALU.mult, ALU.add)
                            step(op)
                            step.wait()
                            step(nc.vector.tensor_scalar(turns[:, :, :, :], turns[:, :, :, :], 12582912.0, -12582912.0,
                                                         ALU.add, ALU.add))
                            step.wait()
                            for part in TWO_PI:
                                step(nc.vector.scalar_tensor_tensor(out=angle[:, :, :, :], in0=turns[:, :, :, :], scalar=-part,
                                                                    in1=angle[:, :, :, :], op0=ALU.mult, op1=ALU.add))
                                step.wait()
                            step(nc.vector.tensor_scalar(angle[:, 0, :, :], angle[:, 0, :, :], math.pi / 2, None, ALU.add))
                            step.wait()
                            pi = float(np.float32(3.1415925))
                            nc.vector.tensor_scalar(angle[:, :, :, :], angle[:, :, :, :], pi, -pi, ALU.min, ALU.max)\
                                .then_inc(angle_ready, 1)
                    elif stage == "cn":
                        t = m
                        dve.wait_ge(sq_ready, R0 + t + 1)
                        c2 = slice(2 * t, 2 * t + 2)
                        step(nc.vector.tensor_reduce(ssq[:, c2], c_tmp[:, t, :].rearrange("p (v n) -> p v n", v=2),
                                                     AX.X, ALU.add))
                        step.wait()
                        nc.vector.tensor_scalar(ssq[:, c2], ssq[:, c2], 1.0 / 256, RMS_EPS, ALU.mult, ALU.add)\
                            .then_inc(ms_ready, 1)
                        dve.wait_ge(rms_ready, R0 + t + 1)
                        for v in range(2):
                            c = slice(v * 256, v * 256 + 256)
                            op = nc.vector.tensor_scalar(c_nat[:, t, c], banks[t][:, c], rms[:, 2 * t + v:2 * t + v + 1],
                                                         None, ALU.mult)
                        op.then_inc(proj_read, 1)
                    elif stage == "kr":
                        t = m[1]
                        dve.wait_ge(proj_done, P0 + 2 + t + 1)
                        nc.vector.tensor_copy(kr_nat[:, t, :], banks[2 + t][:, 0:32]).then_inc(proj_read, 1)
                    elif stage == "cT":
                        dve.wait_ge(c_hi, m + 1)
                        hi = hT_hi[:, 0:4, m * P:(m + 1) * P]
                        nc.vector.tensor_tensor(hT_lo[:, 0:4, m * P:(m + 1) * P],
                                                c_tmp[:, m, :].rearrange("p (k n) -> p k n", k=4), hi.bitcast(F32),
                                                ALU.subtract).then_inc(cT_ready, 1)
                    elif stage == "qkT":
                        g, t = m
                        dve.wait_ge(qk4_tr, 2 * g + t + 1)
                        for dst, bank in ((mqT, banks[6]), (mkT, banks[7])):
                            nc.vector.tensor_copy(dst[:, g % 2, :, t * P:(t + 1) * P],
                                                  bank[0:96, :].rearrange("p (h n) -> p h n", h=4))\
                                .then_inc(qk4_ready, 1)
                    elif stage == "S":
                        b = m % 2
                        dve.wait_ge(s_done, A0 + m + 1)
                        if m >= 2:
                            dve.wait_ge(s_exp, A0 + m - 1)
                        nc.vector.tensor_reduce(neg_max[:, b, :], banks[2 + b][:, :].rearrange("p (a n) -> p a n", a=2),
                                                AX.X, ALU.max, negate=True).then_inc(s_max, 1)
                    elif stage == "P":
                        dve.wait_ge(p_tr, A0 + m + 1)
                        if m >= 2:
                            dve.wait_ge(pv_done, A0 + m - 1)
                        nc.vector.tensor_copy(mpT[:, m % 2, :], banks[4][:, :]).then_inc(pT_ready, 1)
                        dve.wait_ge(s_exp, A0 + m + 1)
                        if m >= 4:
                            dve.wait_ge(o_att, A0 + m - 3)
                        nc.vector.reciprocal(rden[:, m % 4, :], den[:, m % 4, :]).then_inc(rden_ready, 1)
                    elif stage == "owin":
                        t, half = m
                        out_lo(O0 + 2 * half + t, 4 * half, banks[6 + t], t)
                    for n in mla_split(stage, m):
                        split_lo(base[s] + n, 0)

            def out_lo(n, k0, bank, t):
                dve.wait_ge(o_hi, n + 1)
                hi = hT_hi[:, k0:k0 + 4, t * P:(t + 1) * P]
                nc.vector.tensor_tensor(hT_lo[:, k0:k0 + 4, t * P:(t + 1) * P],
                                        bank[:, :].rearrange("p (k n) -> p k n", k=4), hi.bitcast(F32),
                                        ALU.subtract).then_inc(o_ready, 1)

            def first_step(a):
                k, _, part = first_piece(a)
                if a < FIRST:
                    dve.wait_ge(first_full[a % ADA_RING], 16 * (a // ADA_RING + 1))
                else:
                    a += PIECES
                    dve.wait_ge(ada_full[a % ADA_RING], 16 * ((a - FIRST) // ADA_RING + 1))
                if a > 0:
                    dve.wait_ge(acc_step, a)
                if k == 0 and a < FIRST:
                    nc.vector.tensor_scalar(part, ada_raw[:, a % ADA_RING, :], cond[:, 1, 0:1], None, ALU.mult)\
                        .then_inc(acc_step, 1)
                    return
                nc.vector.scalar_tensor_tensor(out=part, in0=ada_raw[:, a % ADA_RING, :], scalar=cond[:, 1, k:k + 1],
                                               in1=part, op0=ALU.mult, op1=ALU.add).then_inc(acc_step, 1)

            nc.vector.memset(acc_gate0, 0.0).then_inc(acc_init, 1)
            dve.wait_ge(cond_ready, 1)
            for a in range(FIRST):
                first_step(a)
            dve.wait_ge(gate_bias, 16)
            dve.wait_ge(ln_col_tr, 1)
            nc.vector.tensor_copy(ln_col[:, :], G[1][:, 0:112]).then_inc(ln_col_ready, 1)
            dve.wait_ge(ln_col_ready, 1)
            mods(0, T[1])
            split_lo(0, 0)
            enter(0, 0)
            split_lo(1, 0)
            split_lo(2, 0)
            for s, (kind, _, _) in enumerate(subs):
                if kind == "ffn":
                    plan = ada_plan[s]

                    def hidden(t, u):
                        dve.wait_ge(silu_done, u + 1)
                        nc.vector.tensor_tensor(hid[:, t, :], sg[:, t, :], G[t][:, CW:2 * CW], ALU.mult)\
                            .then_inc(hid_ready, 1)

                    def take_lo(t, u):
                        dve.wait_ge(fT_hi_ready, u + 1)
                        nc.vector.tensor_tensor(fT_lo[:, t, :], T[t][:, 0:CW], fT_hi[:, t, :].bitcast(F32),
                                                ALU.subtract).then_inc(fT_ready, 1)

                    hidden(0, ffn_units[s])
                    enter(s, 1, lambda: take_lo(0, ffn_units[s]))

                    def body(c0, i, loop):
                        u = ffn_units[s] + 2 * c0 + 4 * i
                        nxt = base[s] + 3 * (c0 + 1)
                        for t in range(NT):
                            ahead = t == 0 and c0 == 0
                            if not ahead:
                                hidden(t, u + t)
                            if loop is not None and loop < len(plan):
                                for n in range((0, 2)[t], (2, 4)[t]):
                                    ada_piece(plan[loop], 6 * ((c0 - 1) % 5) + n, i)
                            if t == 0 or c0 < NCH - 1:
                                split_lo(nxt + 2 * t, i)
                            if not ahead:
                                take_lo(t, u + t)
                            if t == 0:
                                split_lo(nxt + 1, i)
                                if c0 == NCH - 1:
                                    split_lo(nxt + 2, i)
                                if loop is None and fin_of(s, c0) is not None:
                                    mods(fin_of(s, c0), T[1])
                            if s == 0 and c0 == 5:
                                for a in range(FIRST + 4 * t, FIRST + 4 * t + 4):
                                    first_step(a)
                            if t == 0:
                                if c0 == NCH - 1:
                                    residual(s, 0)
                            if loop is not None and loop < len(plan) and t == 1:
                                for n in range(4, 6):
                                    ada_piece(plan[loop], 6 * ((c0 - 1) % 5) + n, i)
                    ffn_walk(dve, s, body)
                if kind == "hyb":
                    hybrid(s)
                    residual(s, 0)
                if kind == "mla":
                    mla(s)
                    residual(s, 0)
                norm(s, 0)
                if s < last_sub:
                    enter(s + 1, 0)
                residual(s, 1)
                norm(s, 1)
            dve.wait_ge(n_ready, 2 * last_sub + 2)
            dve.wait_ge(ln_rows_in, 32 * (last_sub + 1))
            step(nc.vector.tensor_tensor(x[:, 1, :], x[:, 1, :], ln_rows[:, 0, :], ALU.mult))
            step.wait()
            dve.wait_ge(x_ready, 2 * last_sub + 1)
            nc.vector.tensor_tensor(x[:, 1, :], x[:, 1, :], ln_rows[:, 1, :], ALU.add).then_inc(x_ready, 1)

        @block.tensor
        def _(pe):
            def ada_cols_of(s, bank):
                for v in range(2):
                    pe.wait_ge(acc_step, ada_base(s) + PIECES if s > 0 else (v + 1) * KD)
                    for k in range(KD):
                        mm = nc.tensor.matmul(bank[:, v * KD + k:v * KD + k + 1],
                                              acc[:, v * D + k * P:v * D + (k + 1) * P], ones[:, 0:1],
                                              start=True, stop=True)
                mm.then_inc(ada_cols, 1)

            def ada_gate_of(s, half, bank):
                part = (acc_gate0 if s == 0 else acc[:, 2 * D:3 * D])[:, half * 512:half * 512 + 512]
                mm = nc.tensor.matmul(bank[:, :], ones[:, :], part,
                                      start=True, stop=True)
                mm.then_inc(ada_gate, 1)

            def enter(s, t):
                if s > 0:
                    pe.wait_ge(n_ready, 2 * (s - 1) + t + 1)
                for bank, ks in zip(entry_banks(s, t), ((0, 1, 4, 5), (2, 3, 6, 7))):
                    for k in ks:
                        mm = nc.tensor.transpose(bank[:, turned(k)], x[:, t, k * P:(k + 1) * P], ident[:, :])
                    mm.then_inc(n_tr, 1)

            def product(dst, a_hi, a_lo, b_hi, b_lo, start, stop, before=None):
                mm = nc.tensor.matmul(dst, a_hi, b_hi, start=start, stop=False)
                if before is not None:
                    mm.then_inc(before, 1)
                nc.tensor.matmul(dst, a_lo, b_hi, start=False, stop=False)
                return nc.tensor.matmul(dst, a_hi, b_lo, start=False, stop=stop)

            def slot_wait(j0, i):
                pe.wait_ge(lo_ready[j0 % RING], j0 // RING + 1 + i)

            def out_project(s, n, t, slots, inputs):
                j0 = base[s] + slots + n
                if n in inputs:
                    pe.wait_ge(o_ready, inputs[n])
                if t == 0:
                    slot_wait(j0, 0)
                for q in range(2):
                    for half in range(2):
                        k, w = 2 * n + q, slice(q * D + half * 512, q * D + half * 512 + 512)
                        tok = slice(t * P, (t + 1) * P)
                        mm = product(Y[t][half][:, :], hT_hi[:, k, tok], hT_lo[:, k, tok], w_hi[:, j0 % RING, w],
                                     w_lo[:, j0 % RING, w], k == 0, k == KD - 1)
                if n == 3:
                    mm.then_inc(y_ready, 1)
                    if t == 1:
                        pe.wait_ge(y_ready, 2 * s + 2)
                        pe.sem_inc(slot_used, 1)
                elif t == 1:
                    mm.then_inc(slot_used, 1)

            def mla(s):
                for stage, m in mla_plan():
                    if stage == "enter":
                        enter(s, m)
                    elif stage in M_SLOT:
                        g, t = m
                        piece = mla_piece(stage, m)
                        width, tiles = {"c": (512, KD), "kr": (32, KD), "uq": (384, 2), "ukv": (512, 2)}[stage]
                        k0 = 2 if stage == "ukv" else 0
                        bank = mla_bank(stage, t)
                        if stage in ("uq", "ukv"):
                            if g == 0:
                                pe.wait_ge(cT_ready, t + 1)
                            pe.wait_ge(proj_read, P0 + max(piece - 1, 4))
                        per = min(tiles, SLOT // width)
                        for k in range(tiles):
                            if stage == "c" and k % 4 == 0:
                                pe.wait_ge(h_ready, 2 * (2 * s + t) + k // 4 + 1)
                            j0 = base[s] + M_SLOT[stage] + 2 * g + k // per
                            if t == 0 and k % per == 0:
                                slot_wait(j0, 0)
                            w = slice(k % per * width, (k % per + 1) * width)
                            tok = slice(t * P, (t + 1) * P)
                            mm = product(bank[:, 0:width], hT_hi[:, k0 + k, tok], hT_lo[:, k0 + k, tok],
                                         w_hi[:, j0 % RING, w], w_lo[:, j0 % RING, w], k == 0, k == tiles - 1)
                            if t == 1 and k % per == per - 1 and k < tiles - 1:
                                mm.then_inc(slot_used, 1)
                        mm.then_inc(proj_done, 1)
                        if t == 1:
                            pe.wait_ge(proj_done, P0 + piece + 1)
                            pe.sem_inc(slot_used, 1)
                    elif stage == "cT":
                        pe.wait_ge(proj_read, P0 + 4)
                        for k in range(4):
                            mm = nc.tensor.transpose(banks[6 + m][:, k * P:(k + 1) * P], c_nat[:, m, k * P:(k + 1) * P],
                                                     ident[:, :])
                        mm.then_inc(c_tr, 1)
                    elif stage == "qkT":
                        g, t = m
                        pe.wait_ge(q_rot, 2 * g + t + 1)
                        pe.wait_ge(kr_done, 2)
                        pe.wait_ge(proj_read, P0 + mla_piece("ukv", m) + 1)
                        if 2 * g + t > 0:
                            pe.wait_ge(qk4_ready, 2 * (2 * g + t))
                        for bank, src in ((banks[6], q_nat), (banks[7], k_nat)):
                            for h in range(4):
                                mm = nc.tensor.transpose(bank[0:96, h * P:(h + 1) * P], src[:, t, h, :], ident[:, :])
                        mm.then_inc(qk4_tr, 1)
                    elif stage == "S":
                        g, t, p = m // 4, m % 4 // 2, m % 2
                        if m % 4 == 0:
                            pe.wait_ge(qk4_ready, 4 * g + 4)
                        if m >= 2:
                            pe.wait_ge(s_exp, A0 + m - 1)
                        for a in range(2):
                            h = 2 * p + a
                            mm = nc.tensor.matmul(banks[2 + m % 2][:, a * SEQ:(a + 1) * SEQ],
                                                  mqT[:, g % 2, h, t * P:(t + 1) * P], mkT[:, g % 2, h, :],
                                                  start=True, stop=True)
                        mm.then_inc(s_done, 1)
                    elif stage == "P":
                        pe.wait_ge(s_exp, A0 + m + 1)
                        if m > 0:
                            pe.wait_ge(pT_ready, A0 + m)
                        for a in range(2):
                            for kt in range(NT):
                                c = (2 * a + kt) * P
                                mm = nc.tensor.transpose(banks[4][:, c:c + P], mP[:, m % 2, a, kt * P:(kt + 1) * P],
                                                         ident[:, :])
                        mm.then_inc(p_tr, 1)
                    elif stage == "V":
                        g, t, p = m // 4, m % 4 // 2, m % 2
                        pe.wait_ge(pT_ready, A0 + m + 1)
                        if m > 0:
                            pe.wait_ge(o_att, A0 + m)
                        for a in range(2):
                            h = 2 * p + a
                            for kt in range(NT):
                                c = (2 * a + kt) * P
                                mm = nc.tensor.matmul(banks[5][:, a * 64:a * 64 + 64], mpT[:, m % 2, c:c + P],
                                                      v_nat[:, g % 2, kt, h * 64:h * 64 + 64],
                                                      start=kt == 0, stop=kt == 1)
                        mm.then_inc(pv_done, 1)
                    elif stage == "owin":
                        t, half = m
                        pe.wait_ge(o_att, A0 + (8 if half == 0 else 14 + 2 * t))
                        if half == 0:
                            pe.wait_ge(qk4_ready, 16)
                        else:
                            pe.wait_ge(o_ready, O0 + t + 1)
                        for k in range(4):
                            c = (4 * half + k) * P
                            mm = nc.tensor.transpose(banks[6 + t][:, k * P:(k + 1) * P], m_o[:, t, c:c + P], ident[:, :])
                        mm.then_inc(o_tr, 1)
                    elif stage == "out":
                        if m == (0, 0):
                            pe.wait_ge(proj_read, P0 + 20)
                        elif m == (0, 1):
                            pe.wait_ge(s_exp, A0 + 16)
                        out_project(s, *m, MOUT, {0: O0 + m[1] + 1, 2: O0 + m[1] + 3})

            def hybrid(s):
                for stage, m in hybrid_plan():
                    if stage == "enter":
                        enter(s, m)
                    elif stage == "proj":
                        g, t = m
                        width = HG[g][1]
                        if g > 0:
                            pe.wait_ge(proj_read, 2 * g + t - 1)
                        per = SLOT // width
                        for k in range(KD):
                            if g == 0 and k % 4 == 0:
                                pe.wait_ge(h_ready, 2 * (2 * s + t) + k // 4 + 1)
                            j0 = base[s] + HG_SLOT[g] + k // per
                            if t == 0 and k % per == 0:
                                slot_wait(j0, 0)
                            w = slice(k % per * width, (k % per + 1) * width)
                            tok = slice(t * P, (t + 1) * P)
                            mm = product(Y[0][t][:, 0:width], hT_hi[:, k, tok], hT_lo[:, k, tok],
                                         w_hi[:, j0 % RING, w], w_lo[:, j0 % RING, w], k == 0, k == KD - 1)
                            if t == 1 and k % per == per - 1 and k < KD - 1:
                                mm.then_inc(slot_used, 1)
                        mm.then_inc(proj_done, 1)
                        if t == 1:
                            pe.wait_ge(proj_done, 2 * g + 2)
                            pe.sem_inc(slot_used, 1)
                    elif stage == "qk":
                        pe.wait_ge(proj_read, 4)
                        for n in range(2):
                            for q in range(2):
                                for t in range(NT):
                                    p = 2 * n + q
                                    mm = nc.tensor.transpose(G[n][:, q * SEQ + t * P:q * SEQ + (t + 1) * P],
                                                             qa[:, t, p * P:(p + 1) * P], ident[:, :])
                            mm.then_inc(qk_tr, 1)
                        for g in range(2):
                            for t in range(NT):
                                mm = nc.tensor.transpose(banks[6][:, g * SEQ + t * P:g * SEQ + (t + 1) * P],
                                                         k_dup[:, t, g, :], ident[:, :])
                        mm.then_inc(qk_tr, 1)
                    elif stage == "S":
                        t, p = divmod(m, 4)
                        if m == 0:
                            pe.wait_ge(qk_act, 2)
                            pe.wait_ge(qk_dve, 1)
                        if m >= 2:
                            pe.wait_ge(s_max, m - 1)
                        for a in range(2):
                            r = slice(64 * a, 64 * a + 64)
                            mm = nc.tensor.matmul(banks[2 + m % 2 * 2 + a][:, 0:SEQ],
                                                  qT[r, p, t * P:(t + 1) * P], kT[r, p // 2, :], start=True, stop=True)
                        mm.then_inc(s_done, 1)
                    elif stage == "P":
                        pe.wait_ge(s_exp, m + 1)
                        if m > 0:
                            pe.wait_ge(pT_ready, m)
                        for a in range(2):
                            for kt in range(NT):
                                c = (2 * a + kt) * P
                                mm = nc.tensor.transpose(banks[6][:, c:c + P], win_s[:, m % 2, a, kt * P:(kt + 1) * P],
                                                         ident[:, :])
                        mm.then_inc(p_tr, 1)
                    elif stage == "V":
                        t, p = divmod(m, 4)
                        pe.wait_ge(pT_ready, m + 1)
                        if m > 0:
                            pe.wait_ge(o_att, m)
                        for a in range(2):
                            for kt in range(NT):
                                c = (2 * a + kt) * P
                                mm = nc.tensor.matmul(banks[7][:, a * 64:a * 64 + 64], win_pT[:, m % 2, c:c + P],
                                                      va[:, kt, p // 2 * 64:p // 2 * 64 + 64],
                                                      start=kt == 0, stop=kt == 1)
                        mm.then_inc(pv_done, 1)
                    elif stage == "owin":
                        pe.wait_ge(o_att, 8)
                        pe.wait_ge(proj_read, 14)
                        for k in range(4):
                            mm = nc.tensor.transpose(banks[m][:, k * P:(k + 1) * P], o_win[:, m, k * P:(k + 1) * P],
                                                     ident[:, :])
                        mm.then_inc(o_tr, 1)
                    elif stage == "cum":
                        d, t = HSTEP[m]
                        pe.wait_ge(logf_ready, m + 1)
                        pe.wait_ge(tri_ready, 1)
                        for n, (mat, b) in enumerate(((1, 4), (0, 5), (2, 6))):
                            if m > 0:
                                pe.wait_ge(heT_dve, 3 * m - 2 + n)
                            nc.tensor.matmul(banks[b][:, :], tri[:, d, mat, :], logf[m], start=True, stop=True)\
                                .then_inc(cum_done, 1)
                        if m > 0:
                            pe.wait_ge(hexp_ready, 5 * m)
                        for h in range(4):
                            mm = nc.tensor.matmul(banks[7][:, 2 * h:2 * h + 2], logf[m][:, h * P:(h + 1) * P],
                                                  half_sel[:, :], start=True, stop=True)
                        mm.then_inc(cum_done, 1)
                    elif stage in ("prod", "turn"):
                        for n, e in ((0, 0), (1, 1)) if stage == "prod" else ((2, 2),):
                            pe.wait_ge((qe_ready, ke_ready, qe_ready)[n], (2 * m + 1, 2 * m + 1, 2 * m + 2)[n])
                            pe.wait_ge(hexp_ready, 5 * m + 2 + n)
                            for h in range(4):
                                mm = nc.tensor.transpose(banks[4 + n][:, h * P:(h + 1) * P],
                                                         hexp[:, e, h * P:(h + 1) * P], ident[:, :])
                            mm.then_inc(he_tr, 1)
                        if stage == "prod":
                            continue
                        pe.wait_ge(heT_dve, 3 * m + 3)
                        if m == 0:
                            pe.wait_ge(o_ready, 2)
                        else:
                            pe.wait_ge(hA_ready, m)
                        for j in range(2):
                            for h in range(4):
                                c = slice(h * P + 64 * j, h * P + 64 * j + 64)
                                mm = nc.tensor.matmul(banks[0][64 * j:64 * j + 64, h * 64:h * 64 + 64],
                                                      hexpT[:, 1, c], hexpT[:, 0, c], start=True, stop=True)
                        mm.then_inc(hA_done, 1)
                    elif stage == "chain":
                        d, t = HSTEP[m]
                        pe.wait_ge(hA_ready, m + 1)
                        pe.wait_ge(ke_ready, 2 * m + 2)
                        for jj in range(2):
                            j = jj if d == 0 else 1 - jj
                            rows = slice(64 * j, 64 * j + 64)
                            first = m < 2 and jj == 0
                            if dS_index(m, jj) is not None:
                                if dS_index(m, jj) > 0:
                                    pe.wait_ge(S_ready, dS_index(m, jj))
                                for h in range(4):
                                    c = slice(h * P, (h + 1) * P)
                                    mm = nc.tensor.matmul(banks[1][:, c], hexp[rows, 3, c], hv[rows, t, c],
                                                          start=True, stop=True)
                                mm.then_inc(dS_done, 1)
                            if not first:
                                pe.wait_ge(S_ready, {(0, 1): 1, (1, 1): 3, (2, 0): 2, (3, 0): 4, (2, 1): 5, (3, 1): 6}[m, jj])
                            for h in range(4):
                                c = slice(h * P, (h + 1) * P)
                                o = banks[2 + t][rows, c]
                                mm = nc.tensor.matmul(o, hA[rows, h, :], hv[rows, t, c], start=m < 2 and h == 0,
                                                      stop=False, skip_group_check=True)
                                if not first:
                                    mm = nc.tensor.matmul(o, hexpT[:, 2, h * P + 64 * j:h * P + 64 * j + 64],
                                                          hS[:, d, c], start=False, stop=False, skip_group_check=True)
                            mm.then_inc(ho_done, 1)
                    elif stage == "hnorm":
                        pe.wait_ge(ho_ready, m + 1)
                        for k in range(4):
                            mm = nc.tensor.transpose(banks[4 + m][:, k * P:(k + 1) * P], hq[:, m, k * P:(k + 1) * P],
                                                     ident[:, :])
                        mm.then_inc(o_tr, 1)
                    elif stage == "out":
                        if m == (0, 0):
                            pe.wait_ge(hA_ready, 4)
                            pe.wait_ge(S_ready, 6)
                        out_project(s, *m, HOUT, {0: 2, 2: 4})

            pe.wait_ge(ident_ready, 3)
            pe.wait_ge(consts_in, 48)
            nc.tensor.transpose(G[1][:, 0:112], ln_nat[:, :], ident[0:112, 0:112]).then_inc(ln_col_tr, 1)
            pe.wait_ge(x_in[0], 16)
            enter(0, 0)
            ada_cols_of(0, T[1])
            pe.wait_ge(mods_ready, 1)
            pe.wait_ge(ln_col_ready, 1)
            pe.wait_ge(x_in[1], 16)
            enter(0, 1)

            for s, (kind, _, _) in enumerate(subs):
                if kind == "ffn":
                    plan = ada_plan[s]

                    def up(t, c0, i, ks):
                        u = ffn_units[s] + 2 * c0 + 4 * i + t
                        for k in ks:
                            j0 = base[s] + 3 * c0 + k // 4
                            if c0 == 0:
                                if k % 4 == 0:
                                    pe.wait_ge(h_ready, 2 * (2 * s + t) + k // 4 + 1)
                            elif k == 0:
                                pe.wait_ge(hid_ready, u - 1)
                            if k % 4 == 0 and t == 0:
                                slot_wait(j0, i)
                            w = slice((k % 4) * 512, (k % 4 + 1) * 512)
                            tok = slice(t * P, (t + 1) * P)
                            mm = product(G[t][:, :], hT_hi[:, k, tok], hT_lo[:, k, tok],
                                         w_hi[:, j0 % RING, w], w_lo[:, j0 % RING, w], k == 0, k == KD - 1)
                            if k == 3 and t == 1:
                                mm.then_inc(slot_used, 1)
                        if ks[-1] == KD - 1:
                            mm.then_inc(gu_done, 1)

                    def turn(t, c0, i, frees_slot=False):
                        pe.wait_ge(hid_ready, ffn_units[s] + 2 * c0 + 4 * i + t + 1)
                        for q in range(2):
                            mm = nc.tensor.transpose(T[t][:, q * P:(q + 1) * P], hid[:, t, q * P:(q + 1) * P],
                                                     ident[:, :])
                            if q == 0 and frees_slot:
                                mm.then_inc(slot_used, 1)
                        mm.then_inc(hid_tr, 1)

                    def down(t, c0, i, frees_slot=False):
                        j0 = base[s] + 3 * c0 + 2
                        pe.wait_ge(fT_ready, ffn_units[s] + 2 * c0 + 4 * i + t + 1)
                        if t == 0:
                            slot_wait(j0, i)
                        for half in range(2):
                            for q in range(2):
                                w = slice(q * D + half * 512, q * D + half * 512 + 512)
                                mm = product(Y[t][half][:, :], fT_hi[:, t, q * P:(q + 1) * P],
                                             fT_lo[:, t, q * P:(q + 1) * P], w_hi[:, j0 % RING, w],
                                             w_lo[:, j0 % RING, w], c0 == 0 and q == 0, c0 == NCH - 1 and q == 1,
                                             slot_used if frees_slot and half == 0 and q == 0 else None)
                        if c0 == NCH - 1:
                            mm.then_inc(y_ready, 1)
                            if t == 1:
                                pe.wait_ge(y_ready, 2 * s + 2)
                                pe.sem_inc(slot_used, 1)
                        elif t == 1:
                            mm.then_inc(slot_used, 1)

                    def body(c0, i, loop):
                        fin = None if loop is not None else fin_of(s, c0)
                        if fin is not None:
                            ada_cols_of(fin, T[1])
                        turn(0, c0, i)
                        if fin is not None:
                            ada_gate_of(fin, 1, G[0])
                        if c0 == 0:
                            down(0, c0, i)
                            up(1, c0, i, range(KD))
                            turn(1, c0, i, frees_slot=True)
                            up(0, c0 + 1, i, range(KD))
                            down(1, c0, i)
                        elif c0 < NCH - 1:
                            up(1, c0, i, range(KD))
                            down(0, c0, i, frees_slot=True)
                            if fin is not None:
                                ada_gate_of(fin, 0, T[0])
                                pe.wait_ge(mods_ready, fin + 1)
                            turn(1, c0, i)
                            if fin is not None:
                                pe.wait_ge(gate_ready, gate_base(fin) + 2)
                            up(0, c0 + 1, i, range(KD))
                            down(1, c0, i)
                            if fin == 1:
                                pe.wait_ge(acc_step, GATE0 + KD)
                                ada_gate_of(0, 1, G[1])
                                ada_gate_of(0, 0, T[1])
                                pe.wait_ge(gate_ready, 4)
                        else:
                            up(1, c0, i, range(4))
                            down(0, c0, i)
                            if fin is not None:
                                ada_gate_of(fin, 0, T[0])
                                pe.wait_ge(mods_ready, fin + 1)
                            up(1, c0, i, range(4, KD))
                            turn(1, c0, i, frees_slot=True)
                            down(1, c0, i)
                            if fin is not None:
                                pe.wait_ge(gate_ready, gate_base(fin) + 2)

                    if s > 0:
                        enter(s, 0)
                    up(0, 0, 0, range(KD))
                    if s > 0:
                        enter(s, 1)
                    ffn_walk(pe, s, body)
                if kind == "hyb":
                    hybrid(s)
                if kind == "mla":
                    mla(s)


_INS = ["x", "c", "positions", "ada_w", "ada_b", "ln_g", "ln_b", "ffn_w_gate", "ffn_w_up", "ffn_w_down",
        "hyb_w_in", "hyb_w_out", "attn_sink", "hgrn_lb_logits", "hgrn_norm_w", "mla_w_down", "mla_q_norm",
        "mla_kv_norm", "mla_w_uq", "mla_w_ukv", "mla_w_out"]


def kernel(**inputs):
    import numpy as _np
    import concourse.bacc as _bacc
    from concourse import mybir as _mybir
    from concourse.bass_utils import run_bass_kernel_spmd as _run

    nc = _bacc.Bacc("TRN2", target_bir_lowering=False, num_devices=1)
    arrays, aps = {}, {}
    for name in _INS:
        a = _np.ascontiguousarray(inputs[name])
        arrays[f"in_{name}_dram"] = a
        aps[name] = nc.dram_tensor(f"in_{name}_dram", a.shape, _mybir.dt.from_np(a.dtype), kind="ExternalInput").ap()
    out = nc.dram_tensor("out_0_dram", (1, SEQ, D), F32, kind="ExternalOutput").ap()
    build(nc, aps, out)
    r = _run(nc, [arrays], core_ids=[0])
    return r.results[0]["out_0_dram"]
```
